# Optimizing a Trainium2 kernel written in Bass

```python
import math
import jax, jax.numpy as jnp
from jax import lax
import numpy as np

D_MODEL = 1024
BATCH = 1
SEQ = 512
DEPTH = 1
DEC_BATCH = 8
DEC_SEQ = 16
PAST_LEN = 512

CHUNK = 64
D_CONV = 1024
CONV_W = 3
N_RET_HEADS = 4
RET_DK = 256
RET_DV = 512
D_RET_QK = N_RET_HEADS * RET_DK
D_RET_V = N_RET_HEADS * RET_DV
D_FF = 2816
ROPE_BASE = 10000.0
LN_EPS = 1e-5
GN_EPS = 1e-6
ALPHA = (2 * DEPTH) ** 0.25
BETA = (8 * DEPTH) ** -0.25
SPLITS = (D_CONV, D_CONV, D_CONV, D_RET_QK, D_RET_QK, D_RET_V, D_RET_V, D_MODEL, D_MODEL)
D_IN = sum(SPLITS)

kernel_name = "hybrid_shortconv_retention_macaron_deepnorm_step"

def layer_norm(x, g, b):
    xf = x.astype(jnp.float32)
    mu = xf.mean(-1, keepdims=True)
    var = jnp.square(xf - mu).mean(-1, keepdims=True)
    return ((xf - mu) * lax.rsqrt(var + LN_EPS)).astype(x.dtype) * g + b

def swiglu(x, w_up, w_down):
    a, b = jnp.split(x @ w_up, 2, axis=-1)
    return (jax.nn.silu(a) * b) @ w_down

def rotary(x, pos):
    half = x.shape[-1] // 2
    inv_freq = ROPE_BASE ** (-jnp.arange(half, dtype=jnp.float32) / half)
    ang = pos[:, None] * inv_freq[None, :]
    cos = jnp.cos(ang)[None, :, None, :].astype(x.dtype)
    sin = jnp.sin(ang)[None, :, None, :].astype(x.dtype)
    x1, x2 = x[..., :half], x[..., half:]
    return jnp.concatenate([x1 * cos - x2 * sin, x1 * sin + x2 * cos], axis=-1)

def retention_log_gamma():
    return jnp.log(1.0 - 2.0 ** (-5.0 - jnp.arange(N_RET_HEADS, dtype=jnp.float32)))

def retention_block(q, k, v, S, lg):
    L = q.shape[1]
    idx = jnp.arange(L, dtype=jnp.float32)
    diff = idx[:, None] - idx[None, :]
    decay = jnp.where(diff[None] >= 0,
                      jnp.exp(lg[:, None, None] * jnp.maximum(diff, 0.0)[None]), 0.0)
    scores = jnp.einsum('blhd,bmhd->bhlm', q, k) * decay[None]
    intra = jnp.einsum('bhlm,bmhe->blhe', scores, v)
    cross_dec = jnp.exp(lg[None, :] * (idx[:, None] + 1.0))
    cross = jnp.einsum('blhd,bhde->blhe', q, S) * cross_dec[None, :, :, None]
    k_dec = k * jnp.exp(lg[None, :] * (L - 1.0 - idx[:, None]))[None, :, :, None]
    S_new = jnp.exp(lg * L)[None, :, None, None] * S + jnp.einsum('blhd,blhe->bhde', k_dec, v)
    return intra + cross, S_new

def retention_seq(q, k, v, S0):
    lg = retention_log_gamma()
    B, T, H, _ = q.shape
    if T <= CHUNK:
        return retention_block(q, k, v, S0, lg)
    n = T // CHUNK

    def to_chunks(a):
        return a.reshape(B, n, CHUNK, H, a.shape[-1]).swapaxes(0, 1)

    def step(S, qkv):
        qc, kc, vc = qkv
        o, S = retention_block(qc, kc, vc, S, lg)
        return S, o

    S_fin, o = lax.scan(step, S0, (to_chunks(q), to_chunks(k), to_chunks(v)))
    o = o.swapaxes(0, 1).reshape(B, T, H, o.shape[-1])
    return o, S_fin

def short_conv(u, buf, w):
    T = u.shape[1]
    ext = jnp.concatenate([buf.astype(u.dtype), u], axis=1)
    y = sum(ext[:, j:j + T] * w[j] for j in range(CONV_W))
    return y, ext[:, -(CONV_W - 1):]

def mixer(x, pos, conv_buf, S0, w_in, conv_w, w_conv_br, w_ret_br, w_out):
    B, T, _ = x.shape
    offsets = np.cumsum(SPLITS)[:-1].tolist()
    cb, cc, ch, q, k, v, g, gc, gr = jnp.split(x @ w_in, offsets, axis=-1)
    yc, new_buf = short_conv(cc * ch, conv_buf, conv_w)
    y_conv = (cb * yc) @ w_conv_br
    qh = rotary(q.reshape(B, T, N_RET_HEADS, RET_DK), pos).astype(jnp.float32)
    kh = (rotary(k.reshape(B, T, N_RET_HEADS, RET_DK), pos) * (RET_DK ** -0.5)).astype(jnp.float32)
    vh = v.reshape(B, T, N_RET_HEADS, RET_DV).astype(jnp.float32)
    o, S_new = retention_seq(qh, kh, vh, S0.astype(jnp.float32))
    mu = o.mean(-1, keepdims=True)
    var = jnp.square(o - mu).mean(-1, keepdims=True)
    o = ((o - mu) * lax.rsqrt(var + GN_EPS)).astype(x.dtype).reshape(B, T, D_RET_V)
    y_ret = (o * jax.nn.silu(g)) @ w_ret_br
    m = jax.nn.sigmoid(gc) * y_conv + jax.nn.sigmoid(gr) * y_ret
    return m @ w_out, new_buf, S_new.astype(x.dtype)

def layer(x, pos, conv_buf, S0, ln1_g, ln1_b, ffn1_w_up, ffn1_w_down, w_in, conv_w, w_conv_br,
          w_ret_br, w_out, ln2_g, ln2_b, ffn2_w_up, ffn2_w_down, ln3_g, ln3_b):
    x = layer_norm(ALPHA * x + 0.5 * swiglu(x, ffn1_w_up, ffn1_w_down), ln1_g, ln1_b)
    h, new_buf, S_new = mixer(x, pos, conv_buf, S0, w_in, conv_w, w_conv_br, w_ret_br, w_out)
    x = layer_norm(ALPHA * x + h, ln2_g, ln2_b)
    x = layer_norm(ALPHA * x + 0.5 * swiglu(x, ffn2_w_up, ffn2_w_down), ln3_g, ln3_b)
    return x, new_buf, S_new

def setup_inputs(seed: int = 0) -> dict:
    key = jax.random.key(seed)
    ks = jax.random.split(key, 24)
    f32 = jnp.float32

    def nrm(k, shape, scale):
        return jax.random.normal(k, shape, f32) * scale

    def gain(k):
        return 1.0 + nrm(k, (DEPTH, D_MODEL), 0.02)

    def bias(k):
        return nrm(k, (DEPTH, D_MODEL), 0.02)

    col_scale = jnp.concatenate([
        jnp.full((n,), BETA if i in (2, 5) else 1.0, f32) for i, n in enumerate(SPLITS)])
    return {
        "x_prompt": nrm(ks[0], (BATCH, SEQ, D_MODEL), 1.0),
        "x_sample": nrm(ks[1], (DEC_BATCH, DEC_SEQ, D_MODEL), 1.0),
        "cache_conv": nrm(ks[2], (DEPTH, DEC_BATCH, CONV_W - 1, D_CONV), 1.0),
        "state_ret": nrm(ks[3], (DEPTH, DEC_BATCH, N_RET_HEADS, RET_DK, RET_DV), 1.0),
        "ln1_g": gain(ks[4]),
        "ln1_b": bias(ks[5]),
        "ffn1_w_up": nrm(ks[6], (DEPTH, D_MODEL, 2 * D_FF), D_MODEL ** -0.5),
        "ffn1_w_down": nrm(ks[7], (DEPTH, D_FF, D_MODEL), BETA * D_FF ** -0.5),
        "w_in": nrm(ks[8], (DEPTH, D_MODEL, D_IN), D_MODEL ** -0.5) * col_scale,
        "conv_w": nrm(ks[9], (DEPTH, CONV_W, D_CONV), CONV_W ** -0.5),
        "w_conv_br": nrm(ks[10], (DEPTH, D_CONV, D_MODEL), BETA * D_CONV ** -0.5),
        "w_ret_br": nrm(ks[11], (DEPTH, D_RET_V, D_MODEL), BETA * D_RET_V ** -0.5),
        "w_out": nrm(ks[12], (DEPTH, D_MODEL, D_MODEL), BETA * D_MODEL ** -0.5),
        "ln2_g": gain(ks[13]),
        "ln2_b": bias(ks[14]),
        "ffn2_w_up": nrm(ks[15], (DEPTH, D_MODEL, 2 * D_FF), D_MODEL ** -0.5),
        "ffn2_w_down": nrm(ks[16], (DEPTH, D_FF, D_MODEL), BETA * D_FF ** -0.5),
        "ln3_g": gain(ks[17]),
        "ln3_b": bias(ks[18]),
    }

def reference(x_prompt, x_sample, cache_conv, state_ret, ln1_g, ln1_b, ffn1_w_up, ffn1_w_down,
              w_in, conv_w, w_conv_br, w_ret_br, w_out, ln2_g, ln2_b, ffn2_w_up, ffn2_w_down,
              ln3_g, ln3_b):
    Bp, Tp, _ = x_prompt.shape
    Ts = x_sample.shape[1]
    pos_p = jnp.arange(Tp, dtype=jnp.float32)
    pos_s = PAST_LEN + jnp.arange(Ts, dtype=jnp.float32)
    yp, ys = x_prompt, x_sample
    conv_p, ret_p, conv_s, ret_s = [], [], [], []
    for l in range(DEPTH):
        params = (ln1_g[l], ln1_b[l], ffn1_w_up[l], ffn1_w_down[l], w_in[l], conv_w[l],
                  w_conv_br[l], w_ret_br[l], w_out[l], ln2_g[l], ln2_b[l], ffn2_w_up[l],
                  ffn2_w_down[l], ln3_g[l], ln3_b[l])
        buf0 = jnp.zeros((Bp, CONV_W - 1, D_CONV), x_prompt.dtype)
        S0 = jnp.zeros((Bp, N_RET_HEADS, RET_DK, RET_DV), jnp.float32)
        yp, cbp, sp = layer(yp, pos_p, buf0, S0, *params)
        ys, cbs, ss = layer(ys, pos_s, cache_conv[l], state_ret[l], *params)
        conv_p.append(cbp)
        ret_p.append(sp)
        conv_s.append(cbs)
        ret_s.append(ss)
    conv_prompt = jnp.stack(conv_p)
    ret_prompt = jnp.stack(ret_p)
    conv_sample = jnp.stack(conv_s)
    ret_sample = jnp.stack(ret_s)
    return (yp, ys, conv_prompt, ret_prompt, conv_sample, ret_sample)


_drawn_inputs = setup_inputs


def setup_inputs(seed=0):
    import zlib

    import numpy as np

    out = dict(_drawn_inputs(seed))
    spreads = {}
    factors = {'ln2_g': 2.717, 'ln2_b': 2.836, 'ln3_g': 2.875, 'ln3_b': 2.903}
    for name, (base, spread) in spreads.items():
        noise = np.random.default_rng([zlib.crc32(name.encode()), seed]).standard_normal(out[name].shape)
        drawn = base * np.exp(spread * noise) if base else spread * noise
        out[name] = __import__('jax').numpy.asarray(drawn.astype(out[name].dtype))
    for name, factor in factors.items():
        out[name] = (out[name] * factor).astype(out[name].dtype)
    return out
```

```python
from contextlib import ExitStack

import concourse.bass as bass
import numpy as np
from concourse import mybir

D = 1024
NP, NS_, TS = 512, 8, 16
NT = NP + NS_ * TS
TT = NT // 128
PT = NP // 128
HALF = NT // 2
KT = D // 128
D_FF = 2816
FT = D_FF // 128
GROUPS = (12, 10)
H, DK, DV = 4, 256, 512
PAST_LEN = 512
ALPHA = 2.0 ** 0.25
LN_EPS, GN_EPS = 1e-5, 1e-6
ROPE_BASE = 10000.0

NRAW, NSPL = 2, 2
FFN_CHUNKS = 2 * FT + FT
HEAD_CHUNKS = 16
CHUNKS = 2 * FFN_CHUNKS + H * HEAD_CHUNKS + 3 * KT + 3 * KT + KT
HEAD_BANKS = 80
HT_S, HT_M, HT_Q, HT_K, HT_G, HT_W = 0, 512, 640, 768, 773, 776


class Count:

    def __init__(self, at=0):
        self.at, self.shift = at, 0

    def __call__(self, more=0):
        return self.shift + (self.at + more) if not isinstance(self.shift, int) else self.at + more + self.shift

    def past(self, n):
        return not isinstance(self.shift, int) or self.at + self.shift >= n

    def add(self, k=1):
        self.at += k


def repeat(eng, times, counts, pers, body, peel=0):
    starts = [c.at for c in counts]

    def once(i):
        for c, s, p in zip(counts, starts, pers):
            c.at, c.shift = s, i * p
        body(i)
        for c, s, p in zip(counts, starts, pers):
            assert c.at - s == p, (c.at - s, p)

    for i in range(peel):
        once(i)
    with eng.Fori(peel, times) as i:
        once(i)
    for c, s, p in zip(counts, starts, pers):
        c.at, c.shift = s + p * times, 0


def build_layer(nc, a):
    f32, f32r = mybir.dt.float32, mybir.dt.float32r
    ALU, ACT = mybir.AluOpType, mybir.ActivationFunctionType
    ctx = ExitStack()
    with ctx:
        def sb(name, shape, dt=f32):
            return ctx.enter_context(nc.sbuf_tensor(name, shape, dt))

        def sem(name):
            return ctx.enter_context(nc.semaphore(name))

        z = sb("z", [128, TT, D])
        xh = sb("xh", [128, KT, NT], f32r)
        xl = sb("xl", [128, KT, NT], f32r)
        raw = sb("raw", [128, NRAW, D])
        wh = sb("wh", [128, NSPL, D], f32r)
        wl = sb("wl", [128, NSPL, D], f32r)
        ident = sb("ident", [128, 128])
        mv = sb("mv", [128, TT + 1, 2])
        stats = sb("stats", [128, TT + 1, 12])
        rt = sb("rt", [128, 4, TT + 1])
        convw = sb("convw", [128, 3, KT])
        idle = sb("idle", [128, 8])
        mask8 = sb("mask8", [128, NS_])
        cache = sb("cache", [128, KT, NS_, 2])
        cout = sb("cout", [128, KT, NS_ + 1, 2])
        yr = z[:, :, :].rearrange("p a b -> p (a b)").rearrange("p (a b) -> p a b", a=KT)

        slab = (nc.sbuf_base + 31) // 32 * 32
        end = nc.sbuf_base + nc.sbuf_bytes_remaining

        class Region:

            def __init__(self, at=slab):
                self.at = at

            def take(self, name, shape, dt=f32):
                at = self.at
                self.at += -(-4 * int(np.prod(shape[1:])) // 32) * 32
                assert self.at <= end, (name, self.at, end)
                return nc.alloc_sbuf_tensor_at(name, shape, dt, offset=at)

        fm = Region()
        lng, lnb = fm.take("lng", [128, D]), fm.take("lnb", [128, D])
        after_ln = fm.at
        hh = fm.take("hh", [128, max(GROUPS), NT], f32r)
        hl = fm.take("hl", [128, max(GROUPS), NT], f32r)
        sig = fm.take("sig", [128, 2, NT])
        h32 = fm.take("h32", [128, 2, NT])
        xin = fm.take("xin", [128, KT, NT])

        hm = Region()
        cos, sin = hm.take("cos", [128, NT]), hm.take("sin", [128, NT])
        ht = hm.take("ht", [128, HT_W])
        state = hm.take("state", [128, 4, 2 * DV])
        og_at = hm.at
        qh, ql = hm.take("qh", [128, 2, NT], f32r), hm.take("ql", [128, 2, NT], f32r)
        kh, kl = hm.take("kh", [128, 2, NT], f32r), hm.take("kl", [128, 2, NT], f32r)
        om = Region(og_at)
        ogh, ogl = om.take("ogh", [128, 4, NT], f32r), om.take("ogl", [128, 4, NT], f32r)
        qx = hm.take("qx", [128, 2, 144])
        vh, vl = hm.take("vh", [128, TT, DV], f32r), hm.take("vl", [128, TT, DV], f32r)
        vs = hm.take("vs", [128, DV])
        kd = hm.take("kd", [128, 2, DK])
        knh, knl = hm.take("knh", [128, TT, DK], f32r), hm.take("knl", [128, TT, DK], f32r)
        kmh, kml = hm.take("kmh", [128, 2, DK], f32r), hm.take("kml", [128, 2, DK], f32r)
        SC0 = [0, 512, 896, 1152, 1280]
        rot_at = hm.at
        sc = hm.take("sc", [128, 1424])
        rot = Region(rot_at).take("rot", [128, 2, NT])
        sch, scl = hm.take("sch", [128, 1280], f32r), hm.take("scl", [128, 1280], f32r)
        sg = hm.take("sg", [128, 4, NT])
        rm = Region(hm.at)
        on = hm.take("on", [128, 3, DV])
        rope = rm.take("rope", [128, 2, NT])
        ogt = hm.take("ogt", [128, 2, 256])
        sp = hm.take("sp", [128, 2, DV])

        cm = Region(after_ln)
        zh, zl = cm.take("zh", [128, KT, NT], f32r), cm.take("zl", [128, KT, NT], f32r)
        mh, ml = cm.take("mh", [128, KT, NT], f32r), cm.take("ml", [128, KT, NT], f32r)
        mm_at = cm.at
        upr = cm.take("upr", [128, 2, NP + 2])
        usm = cm.take("usm", [128, 2 * NS_, TS + 2])
        csb = cm.take("csb", [128, 2, NT])
        cy = cm.take("cy", [128, 2, NT])
        cz = cm.take("cz", [128, 1, NT])

        ps = ctx.enter_context(nc.psum_tensor("ps", [128, 8, 512], f32))

        raw_loaded = [sem(f"raw_loaded{i}") for i in range(NRAW)]
        hi_split = sem("hi_split")
        chunk_split = sem("chunk_split")
        idle_set = sem("idle_set")
        chunk_used = sem("chunk_used")
        psum_full, psum_free = sem("psum_full"), sem("psum_free")
        x_in = [sem("x_in0"), sem("x_in1")]
        consts_in, z_in, ln_in, table_in, rope_in, cache_in = (
            sem(n) for n in ("consts_in", "z_in", "ln_in", "table_in", "rope_in", "cache_in"))
        dve_step = sem("dve_step")
        act_done = sem("act_done")
        x_ready = sem("x_ready")
        h_ready = sem("h_ready")
        z_ready = sem("z_ready")
        root_asked = sem("root_asked")
        head_ready = sem("head_ready")
        keys_masked = sem("keys_masked")
        conv_ready = sem("conv_ready")
        state_in = [sem(f"state_in{i}") for i in range(4)]
        state_out = [sem(f"state_out{i}") for i in range(4)]
        z_saved, y_out, conv_out, sp_out = sem("z_saved"), sem("y_out"), sem("conv_out"), sem("sp_out")
        block = ctx.enter_context(nc.Block())

        def cols(k, w, of):
            return of[:, k * w:(k + 1) * w]

        def pair(b):
            return ps[:, b:b + 2, 0:HALF]

        def two(v):
            return v.rearrange("p (a b) -> p a b", a=2)

        def one(v):
            return v.rearrange("p o k -> p (o k)")

        U_Q, U_K, U_V, U_KT, U_SC, U_G = 0, 4, 8, 13, 18, 22
        U_O0, U_OP, U_SP, U_O1, U_T0, U_TP = 30, 31, 35, 37, 38, 39
        U_S1, U_T1, U_RET, U_S0 = 47, 55, 56, 72
        assert U_S0 + 8 == HEAD_BANKS

        @block.sync
        def _(sync):
            def load(i, j):
                c = i * NRAW + j
                sync.dma_start(raw[:, j, :], one(a["weights"][bass.ds(c, 1)].rearrange("o p k -> p o k"))
                               ).then_inc(raw_loaded[j], 16)

            for j in range(NRAW):
                load(0, j)
            with sync.Fori(1, CHUNKS // NRAW) as i:
                for j in range(NRAW):
                    sync.wait_ge(chunk_split, i * NRAW + (j - NRAW + 1))
                    load(i, j)

        @block.gpsimd
        def _(pool):
            UN = max(NRAW, NSPL)
            assert UN % NRAW == 0 and UN % NSPL == 0 and CHUNKS % UN == 0

            def split(i, j, first=False):
                r, s = j % NRAW, j % NSPL
                pool.wait_ge(raw_loaded[r], i * (16 * UN // NRAW) + 16 * (j // NRAW + 1))
                if not first:
                    pool.wait_ge(chunk_used, i * UN + (j - NSPL + 1))
                pool.tensor_tensor(idle[:, :], idle[:, :], idle[:, :], ALU.mult)
                pool.tensor_scalar(wh[:, s, :], raw[:, r, :], 1.0, 1.0, ALU.mult, ALU.mult).then_inc(hi_split, 1)
                pool.wait_ge(hi_split, i * UN + (j + 1))
                pool.tensor_tensor(wl[:, s, :], raw[:, r, :], wh[:, s, :].bitcast(f32),
                                   ALU.subtract).then_inc(chunk_split, 1)

            pool.memset(idle[:, :], 0.0).then_inc(idle_set, 1)
            pool.wait_ge(idle_set, 1)
            for j in range(UN):
                split(0, j, first=j < NSPL)
            with pool.Fori(1, CHUNKS // UN) as i:
                for j in range(UN):
                    split(i, j)

        @block.tensor
        def _(pe):
            ck, bk, hr, zr, hd, km = (Count() for _ in range(6))
            owed = [False]

            def loop(times, counts, pers, body, peel=0):
                def checked(i):
                    before = owed[0]
                    body(i)
                    assert isinstance(i, int) or owed[0] == before
                repeat(pe, times, counts, pers, checked, peel)

            def mm(out, lhs, rhs, start, stop):
                ins = nc.tensor.matmul(out, lhs, rhs, start=start, stop=stop)
                if owed[0]:
                    owed[0] = False
                    ins.then_inc(chunk_used, 1)
                return ins

            def mm3(out, lhs, rhs, start, stop):
                mm(out, lhs[1], rhs[0], start, False)
                mm(out, lhs[0], rhs[1], False, False)
                return mm(out, lhs[0], rhs[0], False, stop)

            def bank(n=1):
                b = bk.at % 8
                if bk.past(8):
                    pe.wait_ge(psum_free, bk(n - 8))
                bk.add(n)
                return b

            def chunk():
                s = ck.at % NSPL
                ck.add()
                pe.wait_ge(chunk_split, ck())
                return s

            def unit(w_of, x_hi, x_lo, kts, x_waits=()):
                b = bank(2)
                for half in range(2):
                    if x_waits:
                        x_waits[half]()
                    c = slice(half * HALF, (half + 1) * HALF)
                    for k in range(kts):
                        last = mm3(ps[:, b + half, 0:HALF], w_of(k), (x_hi[:, k, c], x_lo[:, k, c]),
                                   k == 0, k == kts - 1)
                    last.then_inc(psum_full, 1)

            def unit_of_chunk(x_hi=xh, x_lo=xl, x_waits=()):
                s = chunk()
                unit(lambda k: (cols(k, 128, wh[:, s, :]), cols(k, 128, wl[:, s, :])), x_hi, x_lo, KT, x_waits)
                owed[0] = True

            def natural(n_chunks, l_hi, l_lo, before=None):
                b0 = bk.at
                for c in range(n_chunks):
                    s = chunk()
                    if before:
                        before(c)
                    for kk in range(2):
                        k = 2 * c + kk
                        for t in range(TT):
                            if k == 0:
                                bank()
                            tok = slice(t * 128, (t + 1) * 128)
                            last = mm3(ps[:, (b0 + t) % 8, :], (l_hi[:, k, tok], l_lo[:, k, tok]),
                                       (cols(kk, 512, wh[:, s, :]), cols(kk, 512, wl[:, s, :])),
                                       k == 0, k == 2 * n_chunks - 1)
                            if k == 2 * n_chunks - 1:
                                last.then_inc(psum_full, 1)
                    owed[0] = True

            def ffn(first):
                for g, tiles in enumerate(GROUPS):
                    def up(i):
                        for u in range(4):
                            waits = ()
                            if first and g == 0 and isinstance(i, int) and u == 0:
                                waits = [lambda n=n: pe.wait_ge(x_ready, n + 1) for n in range(2)]
                            unit_of_chunk(x_waits=waits)
                    loop(tiles // 2, (ck, bk), (4, 8), up, peel=int(g == 0))
                    h0 = hr.at
                    for _ in range(2):
                        natural(tiles // 2, hh, hl, lambda c: pe.wait_ge(h_ready, h0 + 2 * c + 2))
                    hr.add(tiles)

            def to_T():
                for t in range(TT):
                    zr.add()
                    pe.wait_ge(z_ready, zr())
                    for q in range(2):
                        b = bank()
                        for k in range(4):
                            last = nc.tensor.transpose(cols(k, 128, ps[:, b, :]),
                                                       cols(4 * q + k, 128, z[:, t, :]), ident[:, :])
                            if owed[0]:
                                owed[0] = False
                                last.then_inc(chunk_used, 1)
                        last.then_inc(psum_full, 1)
                pe.wait_ge(psum_free, bk())

            def transposed(srcs, done=True):
                b = bank()
                for k, src in enumerate(srcs):
                    last = nc.tensor.transpose(cols(k, 128, ps[:, b, :]), src, ident[:, :])
                last.then_inc(psum_full, 1)

            def head_wait():
                hd.add()
                pe.wait_ge(head_ready, hd())

            def state_products():
                for bb in range(4):
                    km.add()
                    pe.wait_ge(keys_masked, km())
                    for d in range(2):
                        b = bank()
                        c = slice(d * 128, (d + 1) * 128)
                        mm3(ps[:, b, :], (kmh[:, bb % 2, c], kml[:, bb % 2, c]),
                            (vh[:, 4, :], vl[:, 4, :]), True, True).then_inc(psum_full, 1)

            def cross(group, i):
                b = bank()
                for bb in range(4):
                    pe.wait_ge(state_in[bb], i * 48 + 16 * (group + 1))
                for d in range(2):
                    for bb in range(4):
                        s = 16 * (4 * group + bb)
                        mm(ps[32 * bb:32 * bb + 32, b, :], qx[:, d, s:s + 32], cols(d, DV, state[:, bb, :]),
                           d == 0, False)
                for bb in range(4):
                    s = SC0[4] + 16 * (4 * group + bb)
                    last = mm(ps[32 * bb:32 * bb + 32, b, :], sc[:, s:s + 32], vs[:, :], False, True)
                last.then_inc(psum_full, 1)

            def head(i):
                u0 = bk.at
                for _ in range(4):
                    unit_of_chunk()
                natural(4, xh, xl)
                head_wait()
                for t in range(TT):
                    transposed([rot[:, k, t * 128:(t + 1) * 128] for k in range(2)])
                for j in range(TT):
                    if j != 4:
                        b = bank()
                    at, q0, n = (0, j * 128, NP - j * 128) if j < 3 else ((j - 3) * 256, (j - 1) * 128, 256)
                    kt = slice(j * 128, (j + 1) * 128)
                    for d in range(2):
                        last = mm3(ps[:, b, at:at + n], (kh[:, d, kt], kl[:, d, kt]),
                                   (qh[:, d, q0:q0 + n], ql[:, d, q0:q0 + n]), d == 0, d == 1)
                    if j != 3:
                        last.then_inc(psum_full, 1)
                for _ in range(4):
                    unit_of_chunk()
                head_wait()
                assert bk.at - u0 == U_O0
                cross(0, i)
                for t in range(PT):
                    b = bank()
                    for j in range(t + 1):
                        c = SC0[j] + (t - j) * 128
                        last = mm3(ps[:, b, :], (sch[:, c:c + 128], scl[:, c:c + 128]),
                                   (vh[:, j, :], vl[:, j, :]), j == 0, j == t)
                    last.then_inc(psum_full, 1)
                for d in range(2):
                    b = bank()
                    c = slice(d * 128, (d + 1) * 128)
                    for j in range(PT):
                        last = mm3(ps[:, b, :], (knh[:, j, c], knl[:, j, c]), (vh[:, j, :], vl[:, j, :]),
                                   j == 0, j == PT - 1)
                    last.then_inc(psum_full, 1)
                cross(1, i)
                n0 = bk.at - U_T0 + U_O0

                def o_wait(use):
                    pe.wait_ge(psum_free, bk(use + 1 - bk.at))
                o_wait(u0 + U_O0)
                transposed([cols(k, 128, on[:, 0, :]) for k in range(4)])
                for t in range(PT):
                    o_wait(u0 + U_OP + t)
                    for dp in range(2):
                        transposed([cols(2 * dp + k, 128, on[:, (t + 1) % 3, :]) for k in range(2)])
                state_products()
                o_wait(u0 + U_O1)
                transposed([cols(k, 128, on[:, 2, :]) for k in range(4)])
                head_wait()
                for _ in range(4):
                    s = chunk()
                    for u in range(2):
                        unit(lambda k: (cols(2 * k + u, 128, wh[:, s, :]), cols(2 * k + u, 128, wl[:, s, :])),
                             ogh, ogl, 4)
                    owed[0] = True
                state_products()

            ffn(True)
            pe.wait_ge(consts_in, 32)
            to_T()
            loop(H, (ck, bk, hd, km), (HEAD_CHUNKS, HEAD_BANKS, 3, 8), head)

            def conv(i):
                for _ in range(12):
                    unit_of_chunk()
            loop(2, (ck, bk), (12, 24), conv, peel=1)

            def merge(i):
                for _ in range(4):
                    unit_of_chunk()
                    unit_of_chunk()
                    unit_of_chunk(zh, zl)
            pe.wait_ge(conv_ready, KT)
            loop(2, (ck, bk), (12, 24), merge)
            for _ in range(2):
                natural(4, mh, ml, lambda c: pe.wait_ge(conv_ready, KT + 2 * c + 2))
            to_T()
            ffn(False)
            assert ck.at == CHUNKS

        @block.scalar
        def _(act):
            bk, root, ad, sn = Count(), Count(), Count(), Count()

            def result(ins):
                ad.add()
                ins.then_inc(act_done, 1)

            def copy(out, in_, **kw):
                return nc.scalar.activation(out, in_, ACT.Copy, **kw)

            def full(n=1):
                b = bk.at % 8
                bk.add(n)
                act.wait_ge(psum_full, bk())
                return b

            def ln_load(k):
                act.dma_start(lng[:, :], a[f"ln{k}_g"].to_broadcast([128, D])).then_inc(ln_in, 16)
                act.dma_start(lnb[:, :], a[f"ln{k}_b"].to_broadcast([128, D])).then_inc(ln_in, 16)

            def ffn(peel):
                for g, tiles in enumerate(GROUPS):
                    def up(i):
                        for u in range(2):
                            b = full(2)
                            if bk.past(7):
                                act.wait_ge(psum_free, bk(-6))
                            result(nc.scalar.activation(two(sig[:, u, :]), pair(b), ACT.Sigmoid))
                            bk.add(2)
                    repeat(act, tiles // 2, (bk, ad), (8, 2), up, peel=peel if g == 0 else 0)
                    bk.add(2 * TT)

            def roots(c0, c1):
                root.add()
                act.wait_ge(root_asked, root())
                result(nc.scalar.activation(rt[:, 1, c0:c1], rt[:, 0, c0:c1], ACT.Sqrt))

            def to_T():
                for t in range(TT):
                    for q in range(2):
                        b = full()
                        result(copy(xh[:, 4 * q:4 * q + 4, t * 128:(t + 1) * 128],
                                    ps[:, b, :].rearrange("p (a b) -> p a b", a=4)))

            for half in range(2):
                c = slice(half * HALF, (half + 1) * HALF)
                act.dma_start(xin[:, :, c], a["x_T"][:, :, c]).then_inc(x_in[half], 16)
            act.dma_start(z[:, 0:PT, :], a["x_prompt"].rearrange("(t p) d -> p t d", p=128)).then_inc(z_in, 16)
            act.dma_start(z[:, PT, :], a["x_sample"]).then_inc(z_in, 16)
            act.dma_start(ident[:, :], a["ident"]).then_inc(consts_in, 16)
            act.dma_start(mask8[:, :], a["mask8"]).then_inc(consts_in, 16)
            act.dma_start(convw[:, :, :], a["conv_w"]).then_inc(cache_in, 16)
            act.dma_start(cache[:, :, :, :], a["cache"]).then_inc(cache_in, 16)
            ln_load(1)
            ffn(1)
            roots(0, TT)
            to_T()
            act.wait_ge(z_ready, TT)
            act.dma_start(a["z_scratch"], z[:, :, :]).then_inc(z_saved, 16)
            act.dma_start(cos[:, :], a["cos"]).then_inc(rope_in, 16)
            act.dma_start(sin[:, :], a["sin"]).then_inc(rope_in, 16)
            act.wait_ge(consts_in, 32)

            def dram_state(t, group, slot, i):
                return a[t][4 * group + slot, bass.ds(i, 1)].rearrange("o (k p) e -> p (o k) e", p=128)

            def state_load(i, group):
                for slot in range(4):
                    act.dma_start(state[:, slot, :].rearrange("p (k e) -> p k e", k=2),
                                  dram_state("state_ret", group, slot, i)).then_inc(state_in[slot], 16)

            def masked_keys(group, u0):
                for bb in range(4):
                    s, st = bb % 2, 4 * group + bb
                    if bb >= 2:
                        act.wait_ge(psum_full, bk(u0 + 2 * (bb - 1) - bk.at))
                    copy(kmh[:, s, :], knh[:, 4, :].bitcast(f32), scale=mask8[:, st:st + 1])
                    copy(kml[:, s, :], knl[:, 4, :].bitcast(f32),
                         scale=mask8[:, st:st + 1]).then_inc(keys_masked, 1)

            def state_store(i, group, u0):
                for slot in range(4):
                    act.wait_ge(psum_free, bk(u0 + 2 * slot + 2 - bk.at))
                    act.dma_start(dram_state("ret_sample", group, slot, i),
                                  state[:, slot, :].rearrange("p (k e) -> p k e", k=2)
                                  ).then_inc(state_out[slot], 16)

            def head(i):
                u0 = bk.at
                if not isinstance(i, int):
                    act.wait_ge(psum_free, bk())
                    for slot in range(4):
                        act.wait_ge(state_out[slot], i * 32)
                act.dma_start(ht[:, :], one(a["tables"][bass.ds(i, 1)].rearrange("o p k -> p o k"))
                              ).then_inc(table_in, 16)
                state_load(i, 0)
                bk.add(U_V)
                for t in range(TT):
                    b = full()
                    result(copy(vh[:, t, :], ps[:, b, :]))
                result(copy(vs[:, :], ps[:, b, :]))
                act.wait_ge(table_in, i * 16 + 16)
                for t in range(TT):
                    b = full()
                    if t >= 2:
                        act.wait_ge(psum_free, bk(-2))
                    result(copy(kd[:, t % 2, :], ps[:, b, 0:DK], scale=ht[:, HT_K + t:HT_K + t + 1]))
                bk.add(U_G - U_SC)
                for u in range(4):
                    b = full(2)
                    result(nc.scalar.activation(two(sg[:, u, :]), pair(b), ACT.Sigmoid))
                full()
                state_load(i, 1)
                roots(0, 5)
                act.wait_ge(psum_free, bk(u0 + U_O1 - bk.at))
                act.dma_start(a["ret_prompt"][bass.ds(i, 1)].rearrange("o (k p) e -> p (o k) e", p=128),
                              sp[:, :, :]).then_inc(sp_out, 16)
                roots(5, 6)
                masked_keys(1, u0 + U_S1)
                state_store(i, 1, u0 + U_S1)
                for slot in range(4):
                    act.wait_ge(state_out[slot], i * 32 + 16)
                state_load(i, 0)
                masked_keys(0, u0 + U_S0)
                state_store(i, 0, u0 + U_S0)
                bk.add(u0 + HEAD_BANKS - bk.at)

            repeat(act, H, (bk, ad, root), (HEAD_BANKS, 6 + 5 + 4 + 2, 2), head, peel=1)
            act.wait_ge(psum_free, bk())
            ln_load(2)

            def conv(i):
                for j in range(4):
                    b = full(2)
                    act.wait_ge(psum_free, bk(-8))
                    result(copy(two(csb[:, j % 2, :]), pair(b)))
                    bk.add(4)
            repeat(act, 2, (bk, ad), (24, 4), conv)

            def merge(i):
                for j in range(4):
                    b = full(2)
                    act.wait_ge(psum_free, bk(-8))
                    nc.scalar.activation(two(csb[:, j % 2, :]), pair(b), ACT.Sigmoid)
                    b = full(2)
                    result(nc.scalar.activation(two(cy[:, j % 2, :]), pair(b), ACT.Sigmoid))
                    bk.add(2)
            repeat(act, 2, (bk, ad), (24, 4), merge)
            act.wait_ge(z_saved, 16)
            act.wait_ge(psum_free, bk())
            act.dma_start(z[:, :, :], a["z_scratch"]).then_inc(z_in, 16)
            act.dma_start(a["conv_state"], cout[:, :, :, :]).then_inc(conv_out, 16)
            bk.add(2 * TT)
            roots(0, TT)
            to_T()
            act.wait_ge(z_ready, 2 * TT)
            ln_load(3)
            ffn(0)
            roots(0, TT)
            for t in range(TT):
                act.wait_ge(z_ready, 2 * TT + t + 1)
                dst = a["y_prompt"][t * 128:(t + 1) * 128, :] if t < PT else a["y_sample"]
                act.dma_start(dst, z[:, t, :]).then_inc(y_out, 16)
            act.wait_ge(y_out, 16 * TT)
            act.wait_ge(conv_out, 16)
            act.wait_ge(sp_out, 16 * H)
            for slot in range(4):
                act.wait_ge(state_out[slot], 32 * H)

        @block.vector
        def _(dve):
            bk, ad, st, hr, zr, root = (Count() for _ in range(6))
            V = nc.vector

            def step(ins):
                st.add()
                ins.then_inc(dve_step, 1)

            def after():
                dve.wait_ge(dve_step, st())

            def full(n=1):
                b = bk.at % 8
                bk.add(n)
                dve.wait_ge(psum_full, bk())
                return b

            def act_result(n=1):
                ad.add(n)
                dve.wait_ge(act_done, ad())

            def tt(out, x, y, op):
                return V.tensor_tensor(out, x, y, op)

            def split(hi, lo, x):
                step(V.tensor_copy(hi, x))
                after()
                return tt(lo, x, hi.bitcast(f32), ALU.subtract)

            def ffn():
                for g, tiles in enumerate(GROUPS):
                    def up(i):
                        for u in range(2):
                            act_result()
                            b = full(2)
                            s = two(sig[:, u, :])
                            tt(s, pair(b), s, ALU.mult).then_inc(psum_free, 2)
                            dve.wait_ge(psum_free, bk())
                            b = full(2)
                            tt(two(h32[:, u, :]), pair(b), s, ALU.mult).then_inc(psum_free, 2)
                            dve.wait_ge(psum_free, bk())
                            f = bass.ds(i * 2 + u, 1)
                            split(one(hh[:, f, :]), one(hl[:, f, :]), h32[:, u, :]).then_inc(h_ready, 1)
                    repeat(dve, tiles // 2, (bk, ad, st), (8, 2, 2), up, peel=0)
                    hr.add(tiles)
                    down(0.5 / ALPHA)

            def down(scale):
                for half in range(2):
                    for t in range(TT):
                        b = full()
                        zt = cols(half, 512, z[:, t, :])
                        V.scalar_tensor_tensor(out=zt, in0=ps[:, b, :], scalar=scale, in1=zt,
                                               op0=ALU.mult, op1=ALU.add).then_inc(psum_free, 1)
                dve.wait_ge(psum_free, bk())

            def inv_root(c0, c1, eps):
                var, r, inv, t = mv[:, c0:c1, 1], rt[:, 1, c0:c1], rt[:, 2, c0:c1], rt[:, 3, c0:c1]
                root.add()
                V.tensor_scalar(rt[:, 0, c0:c1], var, eps, None, ALU.add).then_inc(root_asked, 1)
                act_result()
                step(V.reciprocal(inv, r))
                after()
                step(tt(t, inv, inv, ALU.mult))
                after()
                step(tt(t, t, rt[:, 0, c0:c1], ALU.mult))
                after()
                step(V.tensor_scalar(t, t, -0.5, 1.5, ALU.mult, ALU.add))
                after()
                step(tt(inv, inv, t, ALU.mult))
                after()

            def layer_norm(k):
                for t in range(TT):
                    for half in range(2):
                        step(V.bn_stats(stats[:, t, 6 * half:6 * half + 6], cols(half, 512, z[:, t, :])))
                after()
                for t in range(TT):
                    step(V.bn_aggr(mv[:, t, :], stats[:, t, :]))
                after()
                inv_root(0, TT, LN_EPS / ALPHA ** 2)
                dve.wait_ge(ln_in, 32 * k)
                for t in range(TT):
                    step(V.scalar_tensor_tensor(out=z[:, t, :], in0=z[:, t, :], scalar=mv[:, t, 0:1],
                                                in1=lng[:, :], op0=ALU.subtract, op1=ALU.mult))
                    after()
                    V.scalar_tensor_tensor(out=z[:, t, :], in0=z[:, t, :], scalar=rt[:, 2, t:t + 1],
                                           in1=lnb[:, :], op0=ALU.mult, op1=ALU.add).then_inc(z_ready, 1)

            def to_T():
                for t in range(TT):
                    for q in range(2):
                        b = full()
                        act_result()
                        part = slice(4 * q, 4 * q + 4), slice(t * 128, (t + 1) * 128)
                        tt(xl[:, part[0], part[1]], ps[:, b, :].rearrange("p (a b) -> p a b", a=4),
                           xh[:, part[0], part[1]].bitcast(f32), ALU.subtract).then_inc(psum_free, 1)

            for half in range(2):
                c = slice(half * HALF, (half + 1) * HALF)
                dve.wait_ge(x_in[half], 16)
                split(xh[:, :, c], xl[:, :, c], xin[:, :, c]).then_inc(x_ready, 1)
            dve.wait_ge(z_in, 32)
            ffn()
            layer_norm(1)
            to_T()

            dve.wait_ge(z_saved, 16)
            step(V.memset(yr, 0.0))
            step(V.memset(qx[:, :, 128:144], 0.0))
            step(V.memset(sc[:, 1408:1424], 0.0))
            dve.wait_ge(rope_in, 32)

            def rotate(hi, lo):
                b = full(2)
                step(tt(two(rope[:, 0, :]), pair(b), two(cos[:, :]), ALU.mult))
                tt(two(rope[:, 1, :]), pair(b), two(sin[:, :]), ALU.mult).then_inc(psum_free, 2)
                b = full(2)
                after()
                step(tt(two(rot[:, 0, :]), pair(b), two(sin[:, :]), ALU.mult))
                tt(two(rot[:, 1, :]), pair(b), two(cos[:, :]), ALU.mult).then_inc(psum_free, 2)
                after()
                dve.wait_ge(psum_free, bk())
                step(tt(rot[:, 0, :], rope[:, 0, :], rot[:, 0, :], ALU.subtract))
                step(tt(rot[:, 1, :], rope[:, 1, :], rot[:, 1, :], ALU.add))
                after()
                return split(hi[:, :, :], lo[:, :, :], rot[:, :, :])

            def normalise(b, c, slot):
                V.tensor_scalar(on[:, slot, :], ps[:, b, :], mv[:, c, 0:1], rt[:, 2, c:c + 1],
                                ALU.subtract, ALU.mult).then_inc(psum_free, 1)

            def gate_sample(group):
                b = full()
                rows = ps[:, b, :].rearrange("p (d s r) -> p d s r", d=4, s=4)[:, :, :, 0:TS]
                tok = slice(NP + 64 * group, NP + 64 * group + 64)
                after()
                tt(ogt[:, group, :].rearrange("p (d s r) -> p d s r", d=4, s=4), rows,
                   sg[:, :, tok].rearrange("p d (s r) -> p d s r", s=4), ALU.mult).then_inc(psum_free, 1)
                dve.wait_ge(psum_free, bk())
                step(split(ogh[:, :, tok], ogl[:, :, tok], ogt[:, group, :].rearrange("p (d r) -> p d r", d=4)))

            def head(i):
                u0 = bk.at
                dve.wait_ge(psum_full, bk(2))
                step(rotate(qh, ql))
                dve.wait_ge(table_in, i * 16 + 16)
                for d in range(2):
                    step(tt(qx[:, d, 0:128], rot[:, d, NP:NT], ht[:, HT_Q:HT_Q + 128], ALU.mult))
                rotate(kh, kl).then_inc(head_ready, 1)
                for t in range(TT):
                    b = full()
                    act_result(1 if t < 4 else 2)
                    tt(vl[:, t, :], ps[:, b, :], vh[:, t, :].bitcast(f32), ALU.subtract).then_inc(psum_free, 1)
                for t in range(TT):
                    full()
                    act_result()
                    split(knh[:, t, :], knl[:, t, :], kd[:, t % 2, :]).then_inc(psum_free, 1)
                for j in range(3):
                    b = full()
                    n = NP - 128 * j
                    tt(sc[:, SC0[j]:SC0[j] + n], ps[:, b, 0:n], ht[:, HT_S:HT_S + n],
                       ALU.mult).then_inc(psum_free, 1)
                b = full()
                step(tt(sc[:, SC0[3]:SC0[3] + 128], ps[:, b, 128:256], ht[:, HT_S:HT_S + 128], ALU.mult))
                tt(sc[:, SC0[4]:SC0[4] + 128], ps[:, b, 384:512], ht[:, HT_M:HT_M + 128],
                   ALU.mult).then_inc(psum_free, 1)
                dve.wait_ge(psum_free, bk())
                after()
                split(sch[:, :], scl[:, :], sc[:, 0:1280]).then_inc(head_ready, 1)
                for u in range(4):
                    b = full(2)
                    act_result()
                    tt(two(sg[:, u, :]), pair(b), two(sg[:, u, :]), ALU.mult).then_inc(psum_free, 2)
                banks = []
                for c in range(5):
                    banks.append(full())
                    step(V.bn_stats(stats[:, c, 0:6], ps[:, banks[c], :]))
                after()
                V.memset(rt[:, 3, 0:1], 0.0)
                for c in range(5):
                    step(V.bn_aggr(mv[:, c, :], stats[:, c, 0:6]))
                after()
                inv_root(0, 5, GN_EPS)
                for c, slot in enumerate((0, 1, 2, 0, 1)):
                    if c >= 3:
                        dve.wait_ge(psum_full, bk(u0 + (U_TP if c == 3 else U_TP + 2) - bk.at))
                    normalise(banks[c], c, slot)
                if not isinstance(i, int):
                    dve.wait_ge(sp_out, i * 16)
                for d in range(2):
                    b = full()
                    V.tensor_copy(sp[:, d, :], ps[:, b, :]).then_inc(psum_free, 1)
                b = full()
                step(V.bn_stats(stats[:, 5, 0:6], ps[:, b, :]))
                after()
                V.memset(rt[:, 3, 5:6], 0.0)
                step(V.bn_aggr(mv[:, 5, :], stats[:, 5, 0:6]))
                after()
                inv_root(5, 6, GN_EPS)
                dve.wait_ge(psum_full, bk(u0 + U_TP + 4 - bk.at))
                normalise(b, 5, 2)
                gate_sample(0)
                for t in range(PT):
                    for dp in range(2):
                        b = full()
                        tok, dvs = slice(t * 128, (t + 1) * 128), slice(2 * dp, 2 * dp + 2)
                        tmp = ogt[:, dp, :].rearrange("p (d r) -> p d r", d=2)
                        after()
                        tt(tmp, ps[:, b, 0:256].rearrange("p (d r) -> p d r", d=2), sg[:, dvs, tok],
                           ALU.mult).then_inc(psum_free, 1)
                        dve.wait_ge(psum_free, bk())
                        step(split(ogh[:, dvs, tok], ogl[:, dvs, tok], tmp))

                def new_state(loads):
                    for slot in range(4):
                        dve.wait_ge(state_in[slot], i * 48 + 16 * loads)
                        for d in range(2):
                            b = full()
                            s = cols(d, DV, state[:, slot, :])
                            V.scalar_tensor_tensor(out=s, in0=s, scalar=ht[:, HT_G:HT_G + 1], in1=ps[:, b, :],
                                                   op0=ALU.mult, op1=ALU.add).then_inc(psum_free, 1)
                new_state(2)
                gate_sample(1)
                after()
                V.memset(ht[:, HT_G + 1:HT_G + 2], 0.0).then_inc(head_ready, 1)
                for m in range(KT):
                    b = full(2)
                    tt(two(yr[:, m, :]), pair(b), two(yr[:, m, :]), ALU.add).then_inc(psum_free, 2)
                new_state(3)
            repeat(dve, H, (bk, ad, st, root), (HEAD_BANKS, 17, 62, 2), head, peel=1)

            for slot in range(4):
                dve.wait_ge(state_out[slot], 32 * H)
            dve.wait_ge(sp_out, 16 * H)
            dve.wait_ge(cache_in, 32)
            step(V.memset(upr[:, :, 0:2], 0.0))

            def conv(i):
                for jj in range(4):
                    s, j = jj % 2, i * 4 + jj
                    u, us, y = upr[:, s, :], usm[:, s * NS_:(s + 1) * NS_, :], cy[:, s, :]
                    ys = y[:, NP:NT].rearrange("p (s r) -> p s r", s=NS_)
                    full(2)
                    act_result()
                    b = full(2)
                    step(V.tensor_copy(us[:, :, 0:2],
                                       cache[:, bass.ds(j, 1), :, :].rearrange("p o s r -> p (o s) r")))
                    step(tt(u[:, 2:2 + HALF], csb[:, s, 0:HALF], ps[:, b, 0:HALF], ALU.mult))
                    step(tt(u[:, 2 + HALF:2 + NP], csb[:, s, HALF:NP], ps[:, b + 1, 0:NP - HALF], ALU.mult))
                    tt(us[:, :, 2:2 + TS], csb[:, s, NP:NT].rearrange("p (s r) -> p s r", s=NS_),
                       ps[:, b + 1, NP - HALF:HALF].rearrange("p (s r) -> p s r", s=NS_),
                       ALU.mult).then_inc(psum_free, 4)
                    after()
                    dve.wait_ge(psum_free, bk())

                    def w(n):
                        return convw[:, n, bass.ds(j, 1)]
                    step(V.tensor_scalar(y[:, 0:NP], u[:, 0:NP], w(0), None, ALU.mult))
                    step(V.tensor_scalar(ys, us[:, :, 0:TS], w(0), None, ALU.mult))
                    for n in (1, 2):
                        after()
                        for out, x in ((y[:, 0:NP], u[:, n:n + NP]), (ys, us[:, :, n:n + TS])):
                            step(V.scalar_tensor_tensor(out=out, in0=x, scalar=w(n), in1=out,
                                                        op0=ALU.mult, op1=ALU.add))
                    cj = cout[:, bass.ds(j, 1), :, :].rearrange("p o s r -> p (o s) r")
                    step(V.tensor_copy(cj[:, 0:1, :], u[:, NP:NP + 2].rearrange("p (o r) -> p o r", o=1)))
                    step(V.tensor_copy(cj[:, 1:1 + NS_, :], us[:, :, TS:TS + 2]))
                    after()
                    b = full(2)
                    tt(two(cz[:, 0, :]), pair(b), two(y), ALU.mult).then_inc(psum_free, 2)
                    dve.wait_ge(psum_free, bk())
                    f = bass.ds(j, 1)
                    split(one(zh[:, f, :]), one(zl[:, f, :]), cz[:, 0, :]).then_inc(conv_ready, 1)
            repeat(dve, 2, (bk, ad, st), (24, 4, 48), conv)

            def merge(i):
                for jj in range(4):
                    s, f = jj % 2, bass.ds(i * 4 + jj, 1)
                    full(4)
                    act_result()
                    dve.wait_ge(conv_ready, i * 4 + (KT + jj))
                    tt(cz[:, 0, :], cy[:, s, :], one(yr[:, f, :]), ALU.mult).then_inc(psum_free, 4)
                    dve.wait_ge(psum_free, bk())
                    b = full(2)
                    step(tt(two(csb[:, s, :]), pair(b), two(csb[:, s, :]), ALU.mult))
                    after()
                    tt(cz[:, 0, :], cz[:, 0, :], csb[:, s, :], ALU.add).then_inc(psum_free, 2)
                    dve.wait_ge(psum_free, bk())
                    split(one(mh[:, f, :]), one(ml[:, f, :]), cz[:, 0, :]).then_inc(conv_ready, 1)
            repeat(dve, 2, (bk, ad, st), (24, 4, 8), merge)
            dve.wait_ge(z_in, 48)
            down(1.0 / ALPHA)
            layer_norm(2)
            to_T()
            ffn()
            layer_norm(3)


def decay_tables():
    f = np.float32
    lg = np.log(f(1.0) - f(2.0) ** (f(-5.0) - np.arange(H, dtype=f))).astype(f)
    k = np.arange(128)
    t = np.zeros((H, 128, HT_W), f)
    scale = f(DK ** -0.5)
    for h in range(H):
        diff = np.arange(NP)[None, :] - k[:, None]
        t[h, :, HT_S:HT_S + NP] = np.where(diff >= 0, np.exp(lg[h] * np.maximum(diff, 0).astype(f)), 0) * scale
        diff = k[None, :] - k[:, None]
        inside = (diff >= 0) & (k[None, :] // TS == k[:, None] // TS)
        t[h, :, HT_M:HT_M + 128] = np.where(inside, np.exp(lg[h] * np.maximum(diff, 0).astype(f)), 0) * scale
        t[h, :, HT_Q:HT_Q + 128] = np.exp(lg[h] * (k % TS + 1).astype(f))[None, :]
        for tile in range(PT):
            t[h, :, HT_K + tile] = np.exp(lg[h] * (NP - 1 - (tile * 128 + k)).astype(f)) * scale
        t[h, :, HT_K + PT] = np.exp(lg[h] * (TS - 1 - k % TS).astype(f)) * scale
        t[h, :, HT_G] = np.exp(lg[h] * f(TS))
    return t


def rope_tables():
    f = np.float32
    half = DK // 2
    inv = (f(ROPE_BASE) ** (-np.arange(half, dtype=f) / f(half))).astype(f)
    pos = np.concatenate([np.arange(NP), np.tile(PAST_LEN + np.arange(TS), NS_)]).astype(f)
    ang = (inv[:, None] * pos[None, :]).astype(f)
    return np.cos(ang).astype(f), np.sin(ang).astype(f)


def weight_chunks(ffn1_up, ffn1_down, w_in, w_conv, w_ret, w_out, ffn2_up, ffn2_down):
    out = []

    def tiled(w, cols):
        return w.reshape(-1, 128, cols).transpose(1, 0, 2).reshape(128, -1)

    def t_unit(w, c):
        out.append(tiled(w[:, c:c + 128], 128))

    def natural(w, c, k0, k1):
        for k in range(k0, k1, 2):
            out.append(tiled(w[k * 128:(k + 2) * 128, c:c + 512], 512))

    def ffn(up, down):
        f0 = 0
        for tiles in GROUPS:
            for f in range(f0, f0 + tiles):
                t_unit(up, f * 128)
                t_unit(up, D_FF + f * 128)
            for half in range(2):
                natural(down, half * 512, f0, f0 + tiles)
            f0 += tiles

    cb, cc, ch, q, k, v, g, gc, gr = np.cumsum([0, D, D, D, H * DK, H * DK, H * DV, H * DV, D])
    ffn(ffn1_up, ffn1_down)
    for h in range(H):
        for first in (q + h * DK, k + h * DK):
            t_unit(w_in, first)
            t_unit(w_in, first + 128)
        natural(w_in, v + h * DV, 0, KT)
        for u in range(4):
            t_unit(w_in, g + h * DV + u * 128)
        for m in range(4):
            out.append(tiled(w_ret[h * DV:(h + 1) * DV, m * 256:(m + 1) * 256], 256))
    for j in range(KT):
        for first in (cc, ch, cb):
            t_unit(w_in, first + j * 128)
    for j in range(KT):
        t_unit(w_in, gc + j * 128)
        t_unit(w_in, gr + j * 128)
        t_unit(w_conv, j * 128)
    for half in range(2):
        natural(w_out, half * 512, 0, KT)
    ffn(ffn2_up, ffn2_down)
    return np.stack(out)


def kernel(x_prompt, x_sample, cache_conv, state_ret, ln1_g, ln1_b, ffn1_w_up, ffn1_w_down, w_in, conv_w,
           w_conv_br, w_ret_br, w_out, ln2_g, ln2_b, ffn2_w_up, ffn2_w_down, ln3_g, ln3_b):
    import concourse.bacc as bacc
    from concourse.bass_utils import run_bass_kernel_spmd

    def arr(v):
        return np.ascontiguousarray(np.asarray(v))

    xp, xs = arr(x_prompt)[0], arr(x_sample).reshape(NS_ * TS, D)
    x = np.concatenate([xp, xs])
    cos, sin = rope_tables()
    ins = {
        "x_T": x.T.reshape(KT, 128, NT).transpose(1, 0, 2),
        "x_prompt": xp,
        "x_sample": xs,
        "state_ret": arr(state_ret)[0],
        "cache": arr(cache_conv)[0].reshape(NS_, 2, KT, 128).transpose(3, 2, 0, 1),
        "conv_w": arr(conv_w)[0].reshape(3, KT, 128).transpose(2, 0, 1),
        "weights": weight_chunks(*(arr(w)[0] for w in (ffn1_w_up, ffn1_w_down, w_in, w_conv_br, w_ret_br,
                                                       w_out, ffn2_w_up, ffn2_w_down))),
        "ln1_g": arr(ln1_g), "ln1_b": arr(ln1_b), "ln2_g": arr(ln2_g), "ln2_b": arr(ln2_b),
        "ln3_g": arr(ln3_g), "ln3_b": arr(ln3_b),
        "cos": cos, "sin": sin, "tables": decay_tables(),
        "ident": np.eye(128, dtype=np.float32),
        "mask8": (np.arange(128)[:, None] // TS == np.arange(NS_)[None, :]).astype(np.float32),
    }
    outs = {
        "y_prompt": (NP, D), "y_sample": (NS_ * TS, D), "conv_state": (128, KT, NS_ + 1, 2),
        "ret_prompt": (H, DK, DV), "ret_sample": (NS_, H, DK, DV),
    }
    ins = {k: np.ascontiguousarray(v) for k, v in ins.items()}
    nc = bacc.Bacc("TRN2", target_bir_lowering=False, num_devices=1)
    ins = {f"in_{k}": v for k, v in ins.items()}
    args = {k[3:]: nc.dram_tensor(k, v.shape, mybir.dt.float32, kind="ExternalInput").ap() for k, v in ins.items()}
    args |= {k: nc.dram_tensor(f"out_{k}", s, mybir.dt.float32, kind="ExternalOutput").ap() for k, s in outs.items()}
    args["z_scratch"] = nc.dram_tensor("z_scratch", (128, TT, D), mybir.dt.float32, kind="Internal").ap()
    build_layer(nc, args)
    r = run_bass_kernel_spmd(nc, [ins], core_ids=[0]).results[0]
    r = {k: r[f"out_{k}"] for k in outs}

    conv = r["conv_state"].transpose(2, 3, 1, 0).reshape(NS_ + 1, 2, D)
    return (r["y_prompt"][None], r["y_sample"].reshape(NS_, TS, D), conv[None, 0:1], r["ret_prompt"][None, None],
            conv[None, 1:], r["ret_sample"][None])
```

```python
from contextlib import ExitStack

import concourse.bass as bass
import numpy as np
from concourse import mybir

D = 1024
NP, NS_, TS = 512, 8, 16
NT = NP + NS_ * TS
TT = NT // 128
PT = NP // 128
HALF = NT // 2
KT = D // 128
D_FF = 2816
FT = D_FF // 128
GROUPS = (12, 10)
H, DK, DV = 4, 256, 512
PAST_LEN = 512
ALPHA = 2.0 ** 0.25
LN_EPS, GN_EPS = 1e-5, 1e-6
ROPE_BASE = 10000.0

EARLY = 3
NRAW, NSPL = 2, 2
FFN_CHUNKS = 2 * FT + FT
HEAD_CHUNKS = 16
CHUNKS = 2 * FFN_CHUNKS + H * HEAD_CHUNKS + 3 * KT + 3 * KT + KT
HEAD_BANKS = 80
HT_S, HT_M, HT_Q, HT_K, HT_G, HT_W = 0, 512, 640, 768, 773, 776


class Count:

    def __init__(self, at=0):
        self.at, self.shift = at, 0

    def __call__(self, more=0):
        return self.shift + (self.at + more) if not isinstance(self.shift, int) else self.at + more + self.shift

    def past(self, n):
        return not isinstance(self.shift, int) or self.at + self.shift >= n

    def add(self, k=1):
        self.at += k


def repeat(eng, times, counts, pers, body, peel=0):
    starts = [c.at for c in counts]

    def once(i):
        for c, s, p in zip(counts, starts, pers):
            c.at, c.shift = s, i * p
        body(i)
        for c, s, p in zip(counts, starts, pers):
            assert c.at - s == p, (c.at - s, p)

    for i in range(peel):
        once(i)
    with eng.Fori(peel, times) as i:
        once(i)
    for c, s, p in zip(counts, starts, pers):
        c.at, c.shift = s + p * times, 0


def build_layer(nc, a):
    f32, f32r = mybir.dt.float32, mybir.dt.float32r
    ALU, ACT = mybir.AluOpType, mybir.ActivationFunctionType
    ctx = ExitStack()
    with ctx:
        def sb(name, shape, dt=f32):
            return ctx.enter_context(nc.sbuf_tensor(name, shape, dt))

        def sem(name):
            return ctx.enter_context(nc.semaphore(name))

        z = sb("z", [128, TT, D])
        xh = sb("xh", [128, KT, NT], f32r)
        xl = sb("xl", [128, KT, NT], f32r)
        raw = sb("raw", [128, NRAW, D])
        wh = sb("wh", [128, NSPL, D], f32r)
        wl = sb("wl", [128, NSPL, D], f32r)
        ident = sb("ident", [128, 128])
        mv = sb("mv", [128, TT + 1, 2])
        stats = sb("stats", [128, TT + 1, 12])
        rt = sb("rt", [128, 4, TT + 1])
        convw = sb("convw", [128, 3, KT])
        idle = sb("idle", [128, 8])
        mask8 = sb("mask8", [128, NS_])
        cache = sb("cache", [128, KT, NS_, 2])
        cout = sb("cout", [128, KT, NS_ + 1, 2])
        yr = z[:, :, :].rearrange("p a b -> p (a b)").rearrange("p (a b) -> p a b", a=KT)

        slab = (nc.sbuf_base + 31) // 32 * 32
        end = nc.sbuf_base + nc.sbuf_bytes_remaining

        class Region:

            def __init__(self, at=slab):
                self.at = at

            def take(self, name, shape, dt=f32):
                at = self.at
                self.at += -(-4 * int(np.prod(shape[1:])) // 32) * 32
                assert self.at <= end, (name, self.at, end)
                return nc.alloc_sbuf_tensor_at(name, shape, dt, offset=at)

        fm = Region()
        lng, lnb = fm.take("lng", [128, D]), fm.take("lnb", [128, D])
        after_ln = fm.at
        hh = fm.take("hh", [128, max(GROUPS), NT], f32r)
        hl = fm.take("hl", [128, max(GROUPS), NT], f32r)
        sig = fm.take("sig", [128, 2, NT])
        h32 = fm.take("h32", [128, 2, NT])
        xin = fm.take("xin", [128, KT, NT])

        hm = Region()
        cos, sin = hm.take("cos", [128, NT]), hm.take("sin", [128, NT])
        ht = hm.take("ht", [128, HT_W])
        state = hm.take("state", [128, 4, 2 * DV])
        og_at = hm.at
        qh, ql = hm.take("qh", [128, 2, NT], f32r), hm.take("ql", [128, 2, NT], f32r)
        kh, kl = hm.take("kh", [128, 2, NT], f32r), hm.take("kl", [128, 2, NT], f32r)
        om = Region(og_at)
        ogh, ogl = om.take("ogh", [128, 4, NT], f32r), om.take("ogl", [128, 4, NT], f32r)
        qx = hm.take("qx", [128, 2, 144])
        vh, vl = hm.take("vh", [128, TT, DV], f32r), hm.take("vl", [128, TT, DV], f32r)
        vs = hm.take("vs", [128, DV])
        kd = hm.take("kd", [128, 2, DK])
        knh, knl = hm.take("knh", [128, TT, DK], f32r), hm.take("knl", [128, TT, DK], f32r)
        kmh, kml = hm.take("kmh", [128, 2, DK], f32r), hm.take("kml", [128, 2, DK], f32r)
        SC0 = [0, 512, 896, 1152, 1280]
        rot_at = hm.at
        sc = hm.take("sc", [128, 1424])
        rot = Region(rot_at).take("rot", [128, 2, NT])
        on = Region(hm.at).take("on", [128, 5, DV])
        sch, scl = hm.take("sch", [128, 1280], f32r), hm.take("scl", [128, 1280], f32r)
        rope = Region(hm.at).take("rope", [128, 2, NT])
        sg = hm.take("sg", [128, 4, NT])
        on5 = hm.take("on5", [128, DV])
        ogt = hm.take("ogt", [128, 2, 256])
        sp = hm.take("sp", [128, 2, DV])

        cm = Region(after_ln)
        zh, zl = cm.take("zh", [128, KT, NT], f32r), cm.take("zl", [128, KT, NT], f32r)
        mh, ml = cm.take("mh", [128, KT, NT], f32r), cm.take("ml", [128, KT, NT], f32r)
        mm_at = cm.at
        upr = cm.take("upr", [128, 2, NP + 2])
        usm = cm.take("usm", [128, 2 * NS_, TS + 2])
        csb = cm.take("csb", [128, 2, NT])
        cy = cm.take("cy", [128, 2, NT])
        cz = cm.take("cz", [128, 1, NT])

        ps = ctx.enter_context(nc.psum_tensor("ps", [128, 8, 512], f32))

        raw_loaded = [sem(f"raw_loaded{i}") for i in range(NRAW)]
        hi_split = sem("hi_split")
        chunk_split = sem("chunk_split")
        idle_set = sem("idle_set")
        chunk_used = sem("chunk_used")
        psum_full, psum_free = sem("psum_full"), sem("psum_free")
        x_in = [sem("x_in0"), sem("x_in1")]
        consts_in, z_in, ln_in, table_in, rope_in, cache_in = (
            sem(n) for n in ("consts_in", "z_in", "ln_in", "table_in", "rope_in", "cache_in"))
        dve_step = sem("dve_step")
        act_done = sem("act_done")
        x_ready = sem("x_ready")
        h_ready = sem("h_ready")
        z_ready = sem("z_ready")
        root_asked = sem("root_asked")
        head_ready = sem("head_ready")
        keys_masked = sem("keys_masked")
        conv_ready = sem("conv_ready")
        state_in = [sem(f"state_in{i}") for i in range(4)]
        state_out = [sem(f"state_out{i}") for i in range(4)]
        z_saved, y_out, conv_out, sp_out = sem("z_saved"), sem("y_out"), sem("conv_out"), sem("sp_out")
        block = ctx.enter_context(nc.Block())

        def cols(k, w, of):
            return of[:, k * w:(k + 1) * w]

        def pair(b):
            return ps[:, b:b + 2, 0:HALF]

        def two(v):
            return v.rearrange("p (a b) -> p a b", a=2)

        def one(v):
            return v.rearrange("p o k -> p (o k)")

        U_V, U_SC, U_G, U_O0, U_OP, U_G2 = 8, 18, 22, 26, 27, 31
        U_SP, U_O1, U_G3, U_T0, U_S1, U_S0 = 33, 35, 36, 38, 48, 72
        assert U_S0 + 8 == HEAD_BANKS

        @block.sync
        def _(sync):
            def load(i, j):
                c = i * NRAW + j
                sync.dma_start(raw[:, j, :], one(a["weights"][bass.ds(c, 1)].rearrange("o p k -> p o k"))
                               ).then_inc(raw_loaded[j], 16)

            for j in range(NRAW):
                load(0, j)
            with sync.Fori(1, CHUNKS // NRAW) as i:
                for j in range(NRAW):
                    sync.wait_ge(chunk_split, i * NRAW + (j - NRAW + 1))
                    load(i, j)

        @block.gpsimd
        def _(pool):
            UN = max(NRAW, NSPL)
            assert UN % NRAW == 0 and UN % NSPL == 0 and CHUNKS % UN == 0

            def split(i, j, first=False):
                r, s = j % NRAW, j % NSPL
                pool.wait_ge(raw_loaded[r], i * (16 * UN // NRAW) + 16 * (j // NRAW + 1))
                if not first:
                    pool.wait_ge(chunk_used, i * UN + (j - NSPL + 1))
                pool.tensor_tensor(idle[:, :], idle[:, :], idle[:, :], ALU.mult)
                pool.tensor_scalar(wh[:, s, :], raw[:, r, :], 1.0, 1.0, ALU.mult, ALU.mult).then_inc(hi_split, 1)
                pool.wait_ge(hi_split, i * UN + (j + 1))
                pool.tensor_tensor(wl[:, s, :], raw[:, r, :], wh[:, s, :].bitcast(f32),
                                   ALU.subtract).then_inc(chunk_split, 1)

            pool.memset(idle[:, :], 0.0).then_inc(idle_set, 1)
            pool.wait_ge(idle_set, 1)
            for j in range(UN):
                split(0, j, first=j < NSPL)
            with pool.Fori(1, CHUNKS // UN) as i:
                for j in range(UN):
                    split(i, j)

        @block.tensor
        def _(pe):
            ck, bk, hr, zr, hd, km = (Count() for _ in range(6))
            owed = [False]

            def loop(times, counts, pers, body, peel=0):
                def checked(i):
                    before = owed[0]
                    body(i)
                    assert isinstance(i, int) or owed[0] == before
                repeat(pe, times, counts, pers, checked, peel)

            def mm(out, lhs, rhs, start, stop):
                ins = nc.tensor.matmul(out, lhs, rhs, start=start, stop=stop)
                if owed[0]:
                    owed[0] = False
                    ins.then_inc(chunk_used, 1)
                return ins

            def mm3(out, lhs, rhs, start, stop):
                mm(out, lhs[1], rhs[0], start, False)
                mm(out, lhs[0], rhs[1], False, False)
                return mm(out, lhs[0], rhs[0], False, stop)

            def bank(n=1):
                b = bk.at % 8
                if bk.past(8):
                    pe.wait_ge(psum_free, bk(n - 8))
                bk.add(n)
                return b

            def chunk():
                s = ck.at % NSPL
                ck.add()
                pe.wait_ge(chunk_split, ck())
                return s

            def unit(w_of, x_hi, x_lo, kts, x_waits=()):
                b = bank(2)
                for half in range(2):
                    if x_waits:
                        x_waits[half]()
                    c = slice(half * HALF, (half + 1) * HALF)
                    for k in range(kts):
                        last = mm3(ps[:, b + half, 0:HALF], w_of(k), (x_hi[:, k, c], x_lo[:, k, c]),
                                   k == 0, k == kts - 1)
                    last.then_inc(psum_full, 1)

            def unit_of_chunk(x_hi=xh, x_lo=xl, x_waits=()):
                s = chunk()
                unit(lambda k: (cols(k, 128, wh[:, s, :]), cols(k, 128, wl[:, s, :])), x_hi, x_lo, KT, x_waits)
                owed[0] = True

            def natural(n_chunks, l_hi, l_lo, before=None, ends_stage=False):
                b0 = bk.at

                def product(s, k, t):
                    if k == 0:
                        bank()
                    tok, kk = slice(t * 128, (t + 1) * 128), k % 2
                    last = mm3(ps[:, (b0 + t) % 8, :], (l_hi[:, k, tok], l_lo[:, k, tok]),
                               (cols(kk, 512, wh[:, s, :]), cols(kk, 512, wl[:, s, :])),
                               k == 0, k == 2 * n_chunks - 1)
                    if k == 2 * n_chunks - 1:
                        last.then_inc(psum_full, 1)

                for c in range(n_chunks - 2 * ends_stage):
                    s = chunk()
                    if before:
                        before(c)
                    for kk in range(2):
                        for t in range(TT):
                            product(s, 2 * c + kk, t)
                    owed[0] = True
                if ends_stage:
                    slots = []
                    for tiles in (range(EARLY), range(EARLY, TT)):
                        for n in range(2):
                            c = n_chunks - 2 + n
                            if tiles[0] == 0:
                                slots.append(chunk())
                                before(c)
                            for t in tiles:
                                for kk in range(2):
                                    product(slots[n], 2 * c + kk, t)
                            owed[0] = tiles[0] > 0

            def ffn(first):
                for g, tiles in enumerate(GROUPS):
                    def up(i):
                        starts = not first and g == 0 and isinstance(i, int)
                        if starts:
                            first_units()
                        for u in range(2 * starts, 4):
                            waits = ()
                            if first and g == 0 and isinstance(i, int) and u == 0:
                                waits = [lambda n=n: pe.wait_ge(x_ready, n + 1) for n in range(2)]
                            unit_of_chunk(x_waits=waits)
                    loop(tiles // 2, (ck, bk), (4, 8), up, peel=int(g == 0))
                    h0 = hr.at
                    for half in range(2):
                        natural(tiles // 2, hh, hl, lambda c: pe.wait_ge(h_ready, h0 + 2 * c + 2),
                                ends_stage=g == 1 and half == 1)
                    hr.add(tiles)

            def to_T(tiles):
                for t in tiles:
                    zr.add()
                    pe.wait_ge(z_ready, zr())
                    for q in range(2):
                        b = bank()
                        for k in range(4):
                            last = nc.tensor.transpose(cols(k, 128, ps[:, b, :]),
                                                       cols(4 * q + k, 128, z[:, t, :]), ident[:, :])
                            if owed[0]:
                                owed[0] = False
                                last.then_inc(chunk_used, 1)
                        last.then_inc(psum_full, 1)
                pe.wait_ge(psum_free, bk())

            def begin_stage():
                to_T(range(EARLY))
                bk.add(2 * (TT - EARLY))

            def first_units():
                own = bk.at
                slots = [chunk(), chunk()]
                for half in range(2):
                    if half == 1:
                        bk.at = own - 2 * (TT - EARLY)
                        to_T(range(EARLY, TT))
                    c = slice(half * HALF, (half + 1) * HALF)
                    for u, s in enumerate(slots):
                        if half == 1:
                            bk.add(2)
                        for k in range(KT):
                            last = mm3(ps[:, (own + 2 * u) % 8 + half, 0:HALF],
                                       (cols(k, 128, wh[:, s, :]), cols(k, 128, wl[:, s, :])),
                                       (xh[:, k, c], xl[:, k, c]), k == 0, k == KT - 1)
                        if half == 1:
                            last.then_inc(psum_full, 2)
                            owed[0] = True

            def transposed(srcs, done=True):
                b = bank()
                for k, src in enumerate(srcs):
                    last = nc.tensor.transpose(cols(k, 128, ps[:, b, :]), src, ident[:, :])
                last.then_inc(psum_full, 1)

            def head_wait():
                hd.add()
                pe.wait_ge(head_ready, hd())

            def state_products():
                for bb in range(4):
                    km.add()
                    pe.wait_ge(keys_masked, km())
                    for d in range(2):
                        b = bank()
                        c = slice(d * 128, (d + 1) * 128)
                        mm3(ps[:, b, :], (kmh[:, bb % 2, c], kml[:, bb % 2, c]),
                            (vh[:, 4, :], vl[:, 4, :]), True, True).then_inc(psum_full, 1)

            def cross(group, i):
                b = bank()
                for bb in range(4):
                    pe.wait_ge(state_in[bb], i * 48 + 16 * (group + 1))
                for d in range(2):
                    for bb in range(4):
                        s = 16 * (4 * group + bb)
                        mm(ps[32 * bb:32 * bb + 32, b, :], qx[:, d, s:s + 32], cols(d, DV, state[:, bb, :]),
                           d == 0, False)
                for bb in range(4):
                    s = SC0[4] + 16 * (4 * group + bb)
                    last = mm(ps[32 * bb:32 * bb + 32, b, :], sc[:, s:s + 32], vs[:, :], False, True)
                last.then_inc(psum_full, 1)

            def head(i):
                u0 = bk.at
                starts = isinstance(i, int)
                if starts:
                    first_units()
                for _ in range(2 * starts, 4):
                    unit_of_chunk()
                natural(4, xh, xl)
                head_wait()
                for t in range(TT):
                    transposed([rot[:, k, t * 128:(t + 1) * 128] for k in range(2)])
                for j in range(TT):
                    if j != 4:
                        b = bank()
                    at, q0, n = (0, j * 128, NP - j * 128) if j < 3 else ((j - 3) * 256, (j - 1) * 128, 256)
                    kt = slice(j * 128, (j + 1) * 128)
                    for d in range(2):
                        last = mm3(ps[:, b, at:at + n], (kh[:, d, kt], kl[:, d, kt]),
                                   (qh[:, d, q0:q0 + n], ql[:, d, q0:q0 + n]), d == 0, d == 1)
                    if j != 3:
                        last.then_inc(psum_full, 1)
                for _ in range(2):
                    unit_of_chunk()
                head_wait()
                assert bk.at - u0 == U_O0
                cross(0, i)
                for t in range(PT):
                    b = bank()
                    for j in range(t + 1):
                        c = SC0[j] + (t - j) * 128
                        last = mm3(ps[:, b, :], (sch[:, c:c + 128], scl[:, c:c + 128]),
                                   (vh[:, j, :], vl[:, j, :]), j == 0, j == t)
                    last.then_inc(psum_full, 1)
                assert bk.at - u0 == U_G2
                unit_of_chunk()
                for d in range(2):
                    b = bank()
                    c = slice(d * 128, (d + 1) * 128)
                    for j in range(PT):
                        last = mm3(ps[:, b, :], (knh[:, j, c], knl[:, j, c]), (vh[:, j, :], vl[:, j, :]),
                                   j == 0, j == PT - 1)
                    last.then_inc(psum_full, 1)
                cross(1, i)
                unit_of_chunk()
                assert bk.at - u0 == U_T0

                def o_wait(use):
                    pe.wait_ge(psum_free, bk(u0 + use + 1 - bk.at))
                o_wait(U_O0)
                transposed([cols(k, 128, on[:, 0, :]) for k in range(4)])
                for t in range(PT):
                    o_wait(U_OP + t)
                    for dp in range(2):
                        transposed([cols(2 * dp + k, 128, on[:, 1 + t, :]) for k in range(2)])
                o_wait(U_O1)
                transposed([cols(k, 128, on5[:, :]) for k in range(4)])
                state_products()
                head_wait()
                for _ in range(4):
                    s = chunk()
                    for u in range(2):
                        unit(lambda k: (cols(2 * k + u, 128, wh[:, s, :]), cols(2 * k + u, 128, wl[:, s, :])),
                             ogh, ogl, 4)
                    owed[0] = True
                state_products()

            ffn(True)
            pe.wait_ge(consts_in, 32)
            begin_stage()
            loop(H, (ck, bk, hd, km), (HEAD_CHUNKS, HEAD_BANKS, 3, 8), head, peel=1)

            def conv(i):
                for _ in range(12):
                    unit_of_chunk()
            loop(2, (ck, bk), (12, 24), conv, peel=1)

            def merge(i):
                for _ in range(4):
                    unit_of_chunk()
                    unit_of_chunk()
                    unit_of_chunk(zh, zl)
            pe.wait_ge(conv_ready, KT)
            loop(2, (ck, bk), (12, 24), merge)
            for half in range(2):
                natural(4, mh, ml, lambda c: pe.wait_ge(conv_ready, KT + 2 * c + 2), ends_stage=half == 1)
            begin_stage()
            ffn(False)
            assert ck.at == CHUNKS

        @block.scalar
        def _(act):
            bk, root, ad, sn = Count(), Count(), Count(), Count()

            def result(ins):
                ad.add()
                ins.then_inc(act_done, 1)

            def copy(out, in_, **kw):
                return nc.scalar.activation(out, in_, ACT.Copy, **kw)

            def full(n=1):
                b = bk.at % 8
                bk.add(n)
                act.wait_ge(psum_full, bk())
                return b

            def ln_load(k):
                act.dma_start(lng[:, :], a[f"ln{k}_g"].to_broadcast([128, D])).then_inc(ln_in, 16)
                act.dma_start(lnb[:, :], a[f"ln{k}_b"].to_broadcast([128, D])).then_inc(ln_in, 16)

            def ffn(peel):
                for g, tiles in enumerate(GROUPS):
                    def up(i):
                        for u in range(2):
                            b = full(2)
                            if bk.past(7):
                                act.wait_ge(psum_free, bk(-6))
                            result(nc.scalar.activation(two(sig[:, u, :]), pair(b), ACT.Sigmoid))
                            bk.add(2)
                    repeat(act, tiles // 2, (bk, ad), (8, 2), up, peel=peel if g == 0 else 0)
                    bk.add(2 * TT)

            def roots(c0, c1):
                root.add()
                act.wait_ge(root_asked, root())
                result(nc.scalar.activation(rt[:, 1, c0:c1], rt[:, 0, c0:c1], ACT.Sqrt))

            def roots_and_to_T():
                for tiles in (range(EARLY), range(EARLY, TT)):
                    roots(tiles[0], tiles[-1] + 1)
                    to_T(tiles)

            def to_T(tiles):
                for t in tiles:
                    for q in range(2):
                        b = full()
                        result(copy(xh[:, 4 * q:4 * q + 4, t * 128:(t + 1) * 128],
                                    ps[:, b, :].rearrange("p (a b) -> p a b", a=4)))

            for half in range(2):
                c = slice(half * HALF, (half + 1) * HALF)
                act.dma_start(xin[:, :, c], a["x_T"][:, :, c]).then_inc(x_in[half], 16)
            act.dma_start(z[:, 0:PT, :], a["x_prompt"].rearrange("(t p) d -> p t d", p=128)).then_inc(z_in, 16)
            act.dma_start(z[:, PT, :], a["x_sample"]).then_inc(z_in, 16)
            act.dma_start(ident[:, :], a["ident"]).then_inc(consts_in, 16)
            act.dma_start(mask8[:, :], a["mask8"]).then_inc(consts_in, 16)
            act.dma_start(convw[:, :, :], a["conv_w"]).then_inc(cache_in, 16)
            act.dma_start(cache[:, :, :, :], a["cache"]).then_inc(cache_in, 16)
            ln_load(1)
            ffn(1)
            roots_and_to_T()
            act.wait_ge(z_ready, TT)
            act.dma_start(a["z_scratch"], z[:, :, :]).then_inc(z_saved, 16)
            act.dma_start(cos[:, :], a["cos"]).then_inc(rope_in, 16)
            act.dma_start(sin[:, :], a["sin"]).then_inc(rope_in, 16)
            act.wait_ge(consts_in, 32)

            def dram_state(t, group, slot, i):
                return a[t][4 * group + slot, bass.ds(i, 1)].rearrange("o (k p) e -> p (o k) e", p=128)

            def state_load(i, group):
                for slot in range(4):
                    act.dma_start(state[:, slot, :].rearrange("p (k e) -> p k e", k=2),
                                  dram_state("state_ret", group, slot, i)).then_inc(state_in[slot], 16)

            def masked_keys(group, u0):
                for bb in range(4):
                    s, st = bb % 2, 4 * group + bb
                    if bb >= 2:
                        act.wait_ge(psum_full, bk(u0 + 2 * (bb - 1) - bk.at))
                    copy(kmh[:, s, :], knh[:, 4, :].bitcast(f32), scale=mask8[:, st:st + 1])
                    copy(kml[:, s, :], knl[:, 4, :].bitcast(f32),
                         scale=mask8[:, st:st + 1]).then_inc(keys_masked, 1)

            def state_store(i, group, u0):
                for slot in range(4):
                    act.wait_ge(psum_free, bk(u0 + 2 * slot + 2 - bk.at))
                    act.dma_start(dram_state("ret_sample", group, slot, i),
                                  state[:, slot, :].rearrange("p (k e) -> p k e", k=2)
                                  ).then_inc(state_out[slot], 16)

            def head(i):
                u0 = bk.at
                if not isinstance(i, int):
                    act.wait_ge(psum_free, bk())
                    for slot in range(4):
                        act.wait_ge(state_out[slot], i * 32)
                act.dma_start(ht[:, :], one(a["tables"][bass.ds(i, 1)].rearrange("o p k -> p o k"))
                              ).then_inc(table_in, 16)
                state_load(i, 0)
                bk.add(U_V)
                for t in range(TT):
                    b = full()
                    result(copy(vh[:, t, :], ps[:, b, :]))
                result(copy(vs[:, :], ps[:, b, :]))
                act.wait_ge(table_in, i * 16 + 16)
                for t in range(TT):
                    b = full()
                    if t >= 2:
                        act.wait_ge(psum_free, bk(-2))
                    result(copy(kd[:, t % 2, :], ps[:, b, 0:DK], scale=ht[:, HT_K + t:HT_K + t + 1]))
                bk.add(U_G - U_SC)
                def gate(u):
                    b = full(2)
                    result(nc.scalar.activation(two(sg[:, u, :]), pair(b), ACT.Sigmoid))

                gate(0)
                gate(1)
                full()
                state_load(i, 1)
                roots(0, 5)
                bk.add(U_G2 - U_OP)
                gate(2)
                act.wait_ge(psum_free, bk(u0 + U_O1 - bk.at))
                act.dma_start(a["ret_prompt"][bass.ds(i, 1)].rearrange("o (k p) e -> p (o k) e", p=128),
                              sp[:, :, :]).then_inc(sp_out, 16)
                roots(5, 6)
                bk.add(U_G3 - U_SP)
                gate(3)
                masked_keys(1, u0 + U_S1)
                state_store(i, 1, u0 + U_S1)
                for slot in range(4):
                    act.wait_ge(state_out[slot], i * 32 + 16)
                state_load(i, 0)
                masked_keys(0, u0 + U_S0)
                state_store(i, 0, u0 + U_S0)
                bk.add(u0 + HEAD_BANKS - bk.at)

            repeat(act, H, (bk, ad, root), (HEAD_BANKS, 6 + 5 + 4 + 2, 2), head, peel=1)
            act.wait_ge(psum_free, bk())
            ln_load(2)

            def conv(i):
                for j in range(4):
                    b = full(2)
                    act.wait_ge(psum_free, bk(-8))
                    result(copy(two(csb[:, j % 2, :]), pair(b)))
                    bk.add(4)
            repeat(act, 2, (bk, ad), (24, 4), conv)

            def merge(i):
                for j in range(4):
                    b = full(2)
                    act.wait_ge(psum_free, bk(-8))
                    nc.scalar.activation(two(csb[:, j % 2, :]), pair(b), ACT.Sigmoid)
                    b = full(2)
                    result(nc.scalar.activation(two(cy[:, j % 2, :]), pair(b), ACT.Sigmoid))
                    bk.add(2)
            repeat(act, 2, (bk, ad), (24, 4), merge)
            act.wait_ge(z_saved, 16)
            act.wait_ge(psum_free, bk())
            act.dma_start(z[:, :, :], a["z_scratch"]).then_inc(z_in, 16)
            act.dma_start(a["conv_state"], cout[:, :, :, :]).then_inc(conv_out, 16)
            bk.add(2 * TT)
            roots_and_to_T()
            act.wait_ge(z_ready, 2 * TT)
            ln_load(3)
            ffn(0)
            roots(0, EARLY)
            roots(EARLY, TT)
            for t in range(TT):
                act.wait_ge(z_ready, 2 * TT + t + 1)
                dst = a["y_prompt"][t * 128:(t + 1) * 128, :] if t < PT else a["y_sample"]
                act.dma_start(dst, z[:, t, :]).then_inc(y_out, 16)
            act.wait_ge(y_out, 16 * TT)
            act.wait_ge(conv_out, 16)
            act.wait_ge(sp_out, 16 * H)
            for slot in range(4):
                act.wait_ge(state_out[slot], 32 * H)

        @block.vector
        def _(dve):
            bk, ad, st, hr, zr, root = (Count() for _ in range(6))
            V = nc.vector

            def step(ins):
                st.add()
                ins.then_inc(dve_step, 1)

            def after():
                dve.wait_ge(dve_step, st())

            def full(n=1):
                b = bk.at % 8
                bk.add(n)
                dve.wait_ge(psum_full, bk())
                return b

            def act_result(n=1):
                ad.add(n)
                dve.wait_ge(act_done, ad())

            def tt(out, x, y, op):
                return V.tensor_tensor(out, x, y, op)

            def split(hi, lo, x):
                step(V.tensor_copy(hi, x))
                after()
                return tt(lo, x, hi.bitcast(f32), ALU.subtract)

            def ffn():
                for g, tiles in enumerate(GROUPS):
                    def up(i):
                        for u in range(2):
                            act_result()
                            b = full(2)
                            s = two(sig[:, u, :])
                            tt(s, pair(b), s, ALU.mult).then_inc(psum_free, 2)
                            dve.wait_ge(psum_free, bk())
                            b = full(2)
                            tt(two(h32[:, u, :]), pair(b), s, ALU.mult).then_inc(psum_free, 2)
                            dve.wait_ge(psum_free, bk())
                            f = bass.ds(i * 2 + u, 1)
                            split(one(hh[:, f, :]), one(hl[:, f, :]), h32[:, u, :]).then_inc(h_ready, 1)
                    repeat(dve, tiles // 2, (bk, ad, st), (8, 2, 2), up, peel=0)
                    hr.add(tiles)
                    down(0.5 / ALPHA, 0)
                    if g == 0:
                        down(0.5 / ALPHA, 1)

            def down(scale, half, tiles=range(TT)):
                for t in tiles:
                    b = full()
                    zt = cols(half, 512, z[:, t, :])
                    V.scalar_tensor_tensor(out=zt, in0=ps[:, b, :], scalar=scale, in1=zt,
                                           op0=ALU.mult, op1=ALU.add).then_inc(psum_free, 1)
                dve.wait_ge(psum_free, bk())

            def inv_root(c0, c1, eps):
                var, r, inv, t = mv[:, c0:c1, 1], rt[:, 1, c0:c1], rt[:, 2, c0:c1], rt[:, 3, c0:c1]
                root.add()
                V.tensor_scalar(rt[:, 0, c0:c1], var, eps, None, ALU.add).then_inc(root_asked, 1)
                act_result()
                step(V.reciprocal(inv, r))
                after()
                step(tt(t, inv, inv, ALU.mult))
                after()
                step(tt(t, t, rt[:, 0, c0:c1], ALU.mult))
                after()
                step(V.tensor_scalar(t, t, -0.5, 1.5, ALU.mult, ALU.add))
                after()
                step(tt(inv, inv, t, ALU.mult))
                after()

            def moments(half, tiles):
                for t in tiles:
                    step(V.bn_stats(stats[:, t, 6 * half:6 * half + 6], cols(half, 512, z[:, t, :])))

            def inv_deviation(tiles):
                after()
                for t in tiles:
                    step(V.bn_aggr(mv[:, t, :], stats[:, t, :]))
                after()
                inv_root(tiles[0], tiles[-1] + 1, LN_EPS / ALPHA ** 2)

            def scale_and_shift(tiles):
                for t in tiles:
                    step(V.scalar_tensor_tensor(out=z[:, t, :], in0=z[:, t, :], scalar=mv[:, t, 0:1],
                                                in1=lng[:, :], op0=ALU.subtract, op1=ALU.mult))
                    after()
                    V.scalar_tensor_tensor(out=z[:, t, :], in0=z[:, t, :], scalar=rt[:, 2, t:t + 1],
                                           in1=lnb[:, :], op0=ALU.mult, op1=ALU.add).then_inc(z_ready, 1)

            def end_stage(k, scale, transpose=True):
                early, late = range(EARLY), range(EARLY, TT)
                moments(0, range(TT))
                for t in early:
                    down(scale, 1, [t])
                    moments(1, [t])
                inv_deviation(early)
                dve.wait_ge(ln_in, 32 * k)
                scale_and_shift(early[:2])
                down(scale, 1, late)
                scale_and_shift(early[2:])
                if transpose:
                    to_T(early)
                moments(1, late)
                inv_deviation(late)
                scale_and_shift(late)
                if transpose:
                    to_T(late)

            def to_T(tiles):
                for t in tiles:
                    for q in range(2):
                        b = full()
                        act_result()
                        part = slice(4 * q, 4 * q + 4), slice(t * 128, (t + 1) * 128)
                        tt(xl[:, part[0], part[1]], ps[:, b, :].rearrange("p (a b) -> p a b", a=4),
                           xh[:, part[0], part[1]].bitcast(f32), ALU.subtract).then_inc(psum_free, 1)

            for half in range(2):
                c = slice(half * HALF, (half + 1) * HALF)
                dve.wait_ge(x_in[half], 16)
                split(xh[:, :, c], xl[:, :, c], xin[:, :, c]).then_inc(x_ready, 1)
            dve.wait_ge(z_in, 32)
            ffn()
            end_stage(1, 0.5 / ALPHA)

            dve.wait_ge(z_saved, 16)
            step(V.memset(yr, 0.0))
            step(V.memset(qx[:, :, 128:144], 0.0))
            step(V.memset(sc[:, 1408:1424], 0.0))
            dve.wait_ge(rope_in, 32)

            def rotate(hi, lo):
                b = full(2)
                step(tt(two(rope[:, 0, :]), pair(b), two(cos[:, :]), ALU.mult))
                tt(two(rope[:, 1, :]), pair(b), two(sin[:, :]), ALU.mult).then_inc(psum_free, 2)
                b = full(2)
                after()
                step(tt(two(rot[:, 0, :]), pair(b), two(sin[:, :]), ALU.mult))
                tt(two(rot[:, 1, :]), pair(b), two(cos[:, :]), ALU.mult).then_inc(psum_free, 2)
                after()
                dve.wait_ge(psum_free, bk())
                step(tt(rot[:, 0, :], rope[:, 0, :], rot[:, 0, :], ALU.subtract))
                step(tt(rot[:, 1, :], rope[:, 1, :], rot[:, 1, :], ALU.add))
                after()
                return split(hi[:, :, :], lo[:, :, :], rot[:, :, :])

            def normalise(b, c, out):
                V.tensor_scalar(out, ps[:, b, :], mv[:, c, 0:1], rt[:, 2, c:c + 1],
                                ALU.subtract, ALU.mult).then_inc(psum_free, 1)

            def gate_sample(group):
                b = full()
                rows = ps[:, b, :].rearrange("p (d s r) -> p d s r", d=4, s=4)[:, :, :, 0:TS]
                tok = slice(NP + 64 * group, NP + 64 * group + 64)
                after()
                tt(ogt[:, group, :].rearrange("p (d s r) -> p d s r", d=4, s=4), rows,
                   sg[:, :, tok].rearrange("p d (s r) -> p d s r", s=4), ALU.mult).then_inc(psum_free, 1)
                dve.wait_ge(psum_free, bk())
                step(split(ogh[:, :, tok], ogl[:, :, tok], ogt[:, group, :].rearrange("p (d r) -> p d r", d=4)))

            def head(i):
                u0 = bk.at
                dve.wait_ge(psum_full, bk(2))
                step(rotate(qh, ql))
                dve.wait_ge(table_in, i * 16 + 16)
                for d in range(2):
                    step(tt(qx[:, d, 0:128], rot[:, d, NP:NT], ht[:, HT_Q:HT_Q + 128], ALU.mult))
                rotate(kh, kl).then_inc(head_ready, 1)
                for t in range(TT):
                    b = full()
                    act_result(1 if t < 4 else 2)
                    tt(vl[:, t, :], ps[:, b, :], vh[:, t, :].bitcast(f32), ALU.subtract).then_inc(psum_free, 1)
                for t in range(TT):
                    full()
                    act_result()
                    split(knh[:, t, :], knl[:, t, :], kd[:, t % 2, :]).then_inc(psum_free, 1)
                for j in range(3):
                    b = full()
                    n = NP - 128 * j
                    tt(sc[:, SC0[j]:SC0[j] + n], ps[:, b, 0:n], ht[:, HT_S:HT_S + n],
                       ALU.mult).then_inc(psum_free, 1)
                b = full()
                step(tt(sc[:, SC0[3]:SC0[3] + 128], ps[:, b, 128:256], ht[:, HT_S:HT_S + 128], ALU.mult))
                tt(sc[:, SC0[4]:SC0[4] + 128], ps[:, b, 384:512], ht[:, HT_M:HT_M + 128],
                   ALU.mult).then_inc(psum_free, 1)
                dve.wait_ge(psum_free, bk())
                after()
                split(sch[:, :], scl[:, :], sc[:, 0:1280]).then_inc(head_ready, 1)
                def gate(u):
                    act_result()
                    b = full(2)
                    tt(two(sg[:, u, :]), pair(b), two(sg[:, u, :]), ALU.mult).then_inc(psum_free, 2)

                gate(0)
                gate(1)
                banks = []
                for c in range(5):
                    banks.append(full())
                    step(V.bn_stats(stats[:, c, 0:6], ps[:, banks[c], :]))
                after()
                V.memset(rt[:, 3, 0:1], 0.0)
                for c in range(5):
                    step(V.bn_aggr(mv[:, c, :], stats[:, c, 0:6]))
                after()
                inv_root(0, 5, GN_EPS)
                for c in range(5):
                    normalise(banks[c], c, on[:, c, :])
                gate(2)
                if not isinstance(i, int):
                    dve.wait_ge(sp_out, i * 16)
                for d in range(2):
                    b = full()
                    V.tensor_copy(sp[:, d, :], ps[:, b, :]).then_inc(psum_free, 1)
                b = full()
                step(V.bn_stats(stats[:, 5, 0:6], ps[:, b, :]))
                after()
                V.memset(rt[:, 3, 5:6], 0.0)
                step(V.bn_aggr(mv[:, 5, :], stats[:, 5, 0:6]))
                after()
                inv_root(5, 6, GN_EPS)
                normalise(b, 5, on5[:, :])
                gate(3)
                dve.wait_ge(psum_free, bk())
                gate_sample(0)
                for t in range(PT):
                    for dp in range(2):
                        b = full()
                        tok, dvs = slice(t * 128, (t + 1) * 128), slice(2 * dp, 2 * dp + 2)
                        tmp = ogt[:, dp, :].rearrange("p (d r) -> p d r", d=2)
                        after()
                        tt(tmp, ps[:, b, 0:256].rearrange("p (d r) -> p d r", d=2), sg[:, dvs, tok],
                           ALU.mult).then_inc(psum_free, 1)
                        dve.wait_ge(psum_free, bk())
                        step(split(ogh[:, dvs, tok], ogl[:, dvs, tok], tmp))
                gate_sample(1)
                after()
                V.memset(rt[:, 3, 5:6], 0.0).then_inc(head_ready, 1)

                def new_state(loads):
                    for slot in range(4):
                        dve.wait_ge(state_in[slot], i * 48 + 16 * loads)
                        for d in range(2):
                            b = full()
                            s = cols(d, DV, state[:, slot, :])
                            V.scalar_tensor_tensor(out=s, in0=s, scalar=ht[:, HT_G:HT_G + 1], in1=ps[:, b, :],
                                                   op0=ALU.mult, op1=ALU.add).then_inc(psum_free, 1)
                new_state(2)
                for m in range(KT):
                    b = full(2)
                    tt(two(yr[:, m, :]), pair(b), two(yr[:, m, :]), ALU.add).then_inc(psum_free, 2)
                new_state(3)
            repeat(dve, H, (bk, ad, st, root), (HEAD_BANKS, 17, 62, 2), head, peel=1)

            for slot in range(4):
                dve.wait_ge(state_out[slot], 32 * H)
            dve.wait_ge(sp_out, 16 * H)
            dve.wait_ge(cache_in, 32)
            step(V.memset(upr[:, :, 0:2], 0.0))

            def conv(i):
                for jj in range(4):
                    s, j = jj % 2, i * 4 + jj
                    u, us, y = upr[:, s, :], usm[:, s * NS_:(s + 1) * NS_, :], cy[:, s, :]
                    ys = y[:, NP:NT].rearrange("p (s r) -> p s r", s=NS_)
                    full(2)
                    act_result()
                    b = full(2)
                    step(V.tensor_copy(us[:, :, 0:2],
                                       cache[:, bass.ds(j, 1), :, :].rearrange("p o s r -> p (o s) r")))
                    step(tt(u[:, 2:2 + HALF], csb[:, s, 0:HALF], ps[:, b, 0:HALF], ALU.mult))
                    step(tt(u[:, 2 + HALF:2 + NP], csb[:, s, HALF:NP], ps[:, b + 1, 0:NP - HALF], ALU.mult))
                    tt(us[:, :, 2:2 + TS], csb[:, s, NP:NT].rearrange("p (s r) -> p s r", s=NS_),
                       ps[:, b + 1, NP - HALF:HALF].rearrange("p (s r) -> p s r", s=NS_),
                       ALU.mult).then_inc(psum_free, 4)
                    after()
                    dve.wait_ge(psum_free, bk())

                    def w(n):
                        return convw[:, n, bass.ds(j, 1)]
                    step(V.tensor_scalar(y[:, 0:NP], u[:, 0:NP], w(0), None, ALU.mult))
                    step(V.tensor_scalar(ys, us[:, :, 0:TS], w(0), None, ALU.mult))
                    for n in (1, 2):
                        after()
                        for out, x in ((y[:, 0:NP], u[:, n:n + NP]), (ys, us[:, :, n:n + TS])):
                            step(V.scalar_tensor_tensor(out=out, in0=x, scalar=w(n), in1=out,
                                                        op0=ALU.mult, op1=ALU.add))
                    cj = cout[:, bass.ds(j, 1), :, :].rearrange("p o s r -> p (o s) r")
                    step(V.tensor_copy(cj[:, 0:1, :], u[:, NP:NP + 2].rearrange("p (o r) -> p o r", o=1)))
                    step(V.tensor_copy(cj[:, 1:1 + NS_, :], us[:, :, TS:TS + 2]))
                    after()
                    b = full(2)
                    tt(two(cz[:, 0, :]), pair(b), two(y), ALU.mult).then_inc(psum_free, 2)
                    dve.wait_ge(psum_free, bk())
                    f = bass.ds(j, 1)
                    split(one(zh[:, f, :]), one(zl[:, f, :]), cz[:, 0, :]).then_inc(conv_ready, 1)
            repeat(dve, 2, (bk, ad, st), (24, 4, 48), conv)

            def merge(i):
                for jj in range(4):
                    s, f = jj % 2, bass.ds(i * 4 + jj, 1)
                    full(4)
                    act_result()
                    dve.wait_ge(conv_ready, i * 4 + (KT + jj))
                    tt(cz[:, 0, :], cy[:, s, :], one(yr[:, f, :]), ALU.mult).then_inc(psum_free, 4)
                    dve.wait_ge(psum_free, bk())
                    b = full(2)
                    step(tt(two(csb[:, s, :]), pair(b), two(csb[:, s, :]), ALU.mult))
                    after()
                    tt(cz[:, 0, :], cz[:, 0, :], csb[:, s, :], ALU.add).then_inc(psum_free, 2)
                    dve.wait_ge(psum_free, bk())
                    split(one(mh[:, f, :]), one(ml[:, f, :]), cz[:, 0, :]).then_inc(conv_ready, 1)
            repeat(dve, 2, (bk, ad, st), (24, 4, 8), merge)
            dve.wait_ge(z_in, 48)
            down(1.0 / ALPHA, 0)
            end_stage(2, 1.0 / ALPHA)
            ffn()
            end_stage(3, 0.5 / ALPHA, transpose=False)


def decay_tables():
    f = np.float32
    lg = np.log(f(1.0) - f(2.0) ** (f(-5.0) - np.arange(H, dtype=f))).astype(f)
    k = np.arange(128)
    t = np.zeros((H, 128, HT_W), f)
    scale = f(DK ** -0.5)
    for h in range(H):
        diff = np.arange(NP)[None, :] - k[:, None]
        t[h, :, HT_S:HT_S + NP] = np.where(diff >= 0, np.exp(lg[h] * np.maximum(diff, 0).astype(f)), 0) * scale
        diff = k[None, :] - k[:, None]
        inside = (diff >= 0) & (k[None, :] // TS == k[:, None] // TS)
        t[h, :, HT_M:HT_M + 128] = np.where(inside, np.exp(lg[h] * np.maximum(diff, 0).astype(f)), 0) * scale
        t[h, :, HT_Q:HT_Q + 128] = np.exp(lg[h] * (k % TS + 1).astype(f))[None, :]
        for tile in range(PT):
            t[h, :, HT_K + tile] = np.exp(lg[h] * (NP - 1 - (tile * 128 + k)).astype(f)) * scale
        t[h, :, HT_K + PT] = np.exp(lg[h] * (TS - 1 - k % TS).astype(f)) * scale
        t[h, :, HT_G] = np.exp(lg[h] * f(TS))
    return t


def rope_tables():
    f = np.float32
    half = DK // 2
    inv = (f(ROPE_BASE) ** (-np.arange(half, dtype=f) / f(half))).astype(f)
    pos = np.concatenate([np.arange(NP), np.tile(PAST_LEN + np.arange(TS), NS_)]).astype(f)
    ang = (inv[:, None] * pos[None, :]).astype(f)
    return np.cos(ang).astype(f), np.sin(ang).astype(f)


def weight_chunks(ffn1_up, ffn1_down, w_in, w_conv, w_ret, w_out, ffn2_up, ffn2_down):
    out = []

    def tiled(w, cols):
        return w.reshape(-1, 128, cols).transpose(1, 0, 2).reshape(128, -1)

    def t_unit(w, c):
        out.append(tiled(w[:, c:c + 128], 128))

    def natural(w, c, k0, k1):
        for k in range(k0, k1, 2):
            out.append(tiled(w[k * 128:(k + 2) * 128, c:c + 512], 512))

    def ffn(up, down):
        f0 = 0
        for tiles in GROUPS:
            for f in range(f0, f0 + tiles):
                t_unit(up, f * 128)
                t_unit(up, D_FF + f * 128)
            for half in range(2):
                natural(down, half * 512, f0, f0 + tiles)
            f0 += tiles

    cb, cc, ch, q, k, v, g, gc, gr = np.cumsum([0, D, D, D, H * DK, H * DK, H * DV, H * DV, D])
    ffn(ffn1_up, ffn1_down)
    for h in range(H):
        for first in (q + h * DK, k + h * DK):
            t_unit(w_in, first)
            t_unit(w_in, first + 128)
        natural(w_in, v + h * DV, 0, KT)
        for u in range(4):
            t_unit(w_in, g + h * DV + u * 128)
        for m in range(4):
            out.append(tiled(w_ret[h * DV:(h + 1) * DV, m * 256:(m + 1) * 256], 256))
    for j in range(KT):
        for first in (cc, ch, cb):
            t_unit(w_in, first + j * 128)
    for j in range(KT):
        t_unit(w_in, gc + j * 128)
        t_unit(w_in, gr + j * 128)
        t_unit(w_conv, j * 128)
    for half in range(2):
        natural(w_out, half * 512, 0, KT)
    ffn(ffn2_up, ffn2_down)
    return np.stack(out)


def kernel(x_prompt, x_sample, cache_conv, state_ret, ln1_g, ln1_b, ffn1_w_up, ffn1_w_down, w_in, conv_w,
           w_conv_br, w_ret_br, w_out, ln2_g, ln2_b, ffn2_w_up, ffn2_w_down, ln3_g, ln3_b):
    import concourse.bacc as bacc
    from concourse.bass_utils import run_bass_kernel_spmd

    def arr(v):
        return np.ascontiguousarray(np.asarray(v))

    xp, xs = arr(x_prompt)[0], arr(x_sample).reshape(NS_ * TS, D)
    x = np.concatenate([xp, xs])
    cos, sin = rope_tables()
    ins = {
        "x_T": x.T.reshape(KT, 128, NT).transpose(1, 0, 2),
        "x_prompt": xp,
        "x_sample": xs,
        "state_ret": arr(state_ret)[0],
        "cache": arr(cache_conv)[0].reshape(NS_, 2, KT, 128).transpose(3, 2, 0, 1),
        "conv_w": arr(conv_w)[0].reshape(3, KT, 128).transpose(2, 0, 1),
        "weights": weight_chunks(*(arr(w)[0] for w in (ffn1_w_up, ffn1_w_down, w_in, w_conv_br, w_ret_br,
                                                       w_out, ffn2_w_up, ffn2_w_down))),
        "ln1_g": arr(ln1_g), "ln1_b": arr(ln1_b), "ln2_g": arr(ln2_g), "ln2_b": arr(ln2_b),
        "ln3_g": arr(ln3_g), "ln3_b": arr(ln3_b),
        "cos": cos, "sin": sin, "tables": decay_tables(),
        "ident": np.eye(128, dtype=np.float32),
        "mask8": (np.arange(128)[:, None] // TS == np.arange(NS_)[None, :]).astype(np.float32),
    }
    outs = {
        "y_prompt": (NP, D), "y_sample": (NS_ * TS, D), "conv_state": (128, KT, NS_ + 1, 2),
        "ret_prompt": (H, DK, DV), "ret_sample": (NS_, H, DK, DV),
    }
    ins = {k: np.ascontiguousarray(v) for k, v in ins.items()}
    nc = bacc.Bacc("TRN2", target_bir_lowering=False, num_devices=1)
    ins = {f"in_{k}": v for k, v in ins.items()}
    args = {k[3:]: nc.dram_tensor(k, v.shape, mybir.dt.float32, kind="ExternalInput").ap() for k, v in ins.items()}
    args |= {k: nc.dram_tensor(f"out_{k}", s, mybir.dt.float32, kind="ExternalOutput").ap() for k, s in outs.items()}
    args["z_scratch"] = nc.dram_tensor("z_scratch", (128, TT, D), mybir.dt.float32, kind="Internal").ap()
    build_layer(nc, args)
    r = run_bass_kernel_spmd(nc, [ins], core_ids=[0]).results[0]
    r = {k: r[f"out_{k}"] for k in outs}

    conv = r["conv_state"].transpose(2, 3, 1, 0).reshape(NS_ + 1, 2, D)
    return (r["y_prompt"][None], r["y_sample"].reshape(NS_, TS, D), conv[None, 0:1], r["ret_prompt"][None, None],
            conv[None, 1:], r["ret_sample"][None])
```

```python
from contextlib import ExitStack

import concourse.bass as bass
import numpy as np
from concourse import mybir

D = 1024
NP, NS_, TS = 512, 8, 16
NT = NP + NS_ * TS
TT = NT // 128
PT = NP // 128
HALF = NT // 2
KT = D // 128
D_FF = 2816
FT = D_FF // 128
GROUPS = (12, 10)
H, DK, DV = 4, 256, 512
PAST_LEN = 512
ALPHA = 2.0 ** 0.25
LN_EPS, GN_EPS = 1e-5, 1e-6
ROPE_BASE = 10000.0

EARLY = 3
X_PIECES = [(half, range(k, k + 2)) for half in range(2) for k in range(0, KT, 2)]
NRAW, NSPL = 2, 2
FFN_CHUNKS = 2 * FT + FT
HEAD_CHUNKS = 16
CHUNKS = 2 * FFN_CHUNKS + H * HEAD_CHUNKS + 3 * KT + 3 * KT + KT
HEAD_BANKS = 80
HT_S, HT_M, HT_Q, HT_K, HT_G, HT_W = 0, 512, 640, 768, 773, 776


class Count:

    def __init__(self, at=0):
        self.at, self.shift = at, 0

    def __call__(self, more=0):
        return self.shift + (self.at + more) if not isinstance(self.shift, int) else self.at + more + self.shift

    def past(self, n):
        return not isinstance(self.shift, int) or self.at + self.shift >= n

    def add(self, k=1):
        self.at += k


def repeat(eng, times, counts, pers, body, peel=0):
    starts = [c.at for c in counts]

    def once(i):
        for c, s, p in zip(counts, starts, pers):
            c.at, c.shift = s, i * p
        body(i)
        for c, s, p in zip(counts, starts, pers):
            assert c.at - s == p, (c.at - s, p)

    for i in range(peel):
        once(i)
    with eng.Fori(peel, times) as i:
        once(i)
    for c, s, p in zip(counts, starts, pers):
        c.at, c.shift = s + p * times, 0


def build_layer(nc, a):
    f32, f32r = mybir.dt.float32, mybir.dt.float32r
    ALU, ACT = mybir.AluOpType, mybir.ActivationFunctionType
    ctx = ExitStack()
    with ctx:
        def sb(name, shape, dt=f32):
            return ctx.enter_context(nc.sbuf_tensor(name, shape, dt))

        def sem(name):
            return ctx.enter_context(nc.semaphore(name))

        z = sb("z", [128, TT, D])
        xh = sb("xh", [128, KT, NT], f32r)
        xl = sb("xl", [128, KT, NT], f32r)
        raw = sb("raw", [128, NRAW, D])
        wh = sb("wh", [128, NSPL, D], f32r)
        wl = sb("wl", [128, NSPL, D], f32r)
        ident = sb("ident", [128, 128])
        mv = sb("mv", [128, TT + 1, 2])
        stats = sb("stats", [128, TT + 1, 12])
        rt = sb("rt", [128, 4, TT + 1])
        convw = sb("convw", [128, 3, KT])
        idle = sb("idle", [128, 8])
        odd_even = sb("odd_even", [128, 2])
        cache = sb("cache", [128, KT, NS_, 2])
        cout = sb("cout", [128, KT, NS_ + 1, 2])
        yr = z[:, :, :].rearrange("p a b -> p (a b)").rearrange("p (a b) -> p a b", a=KT)

        slab = (nc.sbuf_base + 31) // 32 * 32
        end = nc.sbuf_base + nc.sbuf_bytes_remaining

        class Region:

            def __init__(self, at=slab):
                self.at = at

            def take(self, name, shape, dt=f32):
                at = self.at
                self.at += -(-4 * int(np.prod(shape[1:])) // 32) * 32
                assert self.at <= end, (name, self.at, end)
                return nc.alloc_sbuf_tensor_at(name, shape, dt, offset=at)

        fm = Region()
        lng, lnb = fm.take("lng", [128, D]), fm.take("lnb", [128, D])
        after_ln = fm.at
        hh = fm.take("hh", [128, max(GROUPS), NT], f32r)
        hl = fm.take("hl", [128, max(GROUPS), NT], f32r)
        sig = fm.take("sig", [128, 2, NT])
        h32 = fm.take("h32", [128, 2, NT])
        xin = fm.take("xin", [128, KT, NT])

        hm = Region()
        cos, sin = hm.take("cos", [128, NT]), hm.take("sin", [128, NT])
        ht = hm.take("ht", [128, HT_W])
        state = hm.take("state", [128, 4, 2 * DV])
        og_at = hm.at
        qh, ql = hm.take("qh", [128, 2, NT], f32r), hm.take("ql", [128, 2, NT], f32r)
        kh, kl = hm.take("kh", [128, 2, NT], f32r), hm.take("kl", [128, 2, NT], f32r)
        om = Region(og_at)
        ogh, ogl = om.take("ogh", [128, 4, NT], f32r), om.take("ogl", [128, 4, NT], f32r)
        qx = hm.take("qx", [128, 2, 144])
        vh, vl = hm.take("vh", [128, PT, DV], f32r), hm.take("vl", [128, PT, DV], f32r)
        vs = hm.take("vs", [128, DV])
        on5 = Region(hm.at).take("on5", [128, DV])
        kd = hm.take("kd", [128, 2, DK])
        knh, knl = hm.take("knh", [128, PT, DK], f32r), hm.take("knl", [128, PT, DK], f32r)
        vp, kp = hm.take("vp", [128, 4, DV], f32r), hm.take("kp", [128, 4, DK], f32r)
        km = hm.take("km", [128, 4, DK], f32r)
        SC0 = [0, 512, 896, 1152, 1280]
        rot_at = hm.at
        ogt = Region(hm.at).take("ogt", [128, 1280])
        sc = hm.take("sc", [128, 1424])
        rot = Region(rot_at).take("rot", [128, 2, NT])
        on = Region(hm.at).take("on", [128, 5, DV])
        sch, scl = hm.take("sch", [128, 1280], f32r), hm.take("scl", [128, 1280], f32r)
        rope = Region(hm.at).take("rope", [128, 2, NT])
        sk = Region(hm.at)
        k4 = [sk.take(n, [128, DK], f32r) for n in ("k4h", "k4l")]
        sv = Region(hm.at + 2 * 4 * NT)
        v4 = [sv.take(n, [128, DV], f32r) for n in ("v4h", "v4l")]
        sg = hm.take("sg", [128, 4, NT])
        sp = hm.take("sp", [128, 2, DV])

        cm = Region(after_ln)
        zh, zl = cm.take("zh", [128, KT, NT], f32r), cm.take("zl", [128, KT, NT], f32r)
        mh, ml = cm.take("mh", [128, KT, NT], f32r), cm.take("ml", [128, KT, NT], f32r)
        mm_at = cm.at
        upr = cm.take("upr", [128, 2, NP + 2])
        usm = cm.take("usm", [128, 2 * NS_, TS + 2])
        csb = cm.take("csb", [128, 2, NT])
        cy = cm.take("cy", [128, 2, NT])
        cz = cm.take("cz", [128, 1, NT])

        ps = ctx.enter_context(nc.psum_tensor("ps", [128, 8, 512], f32))

        raw_loaded = [sem(f"raw_loaded{i}") for i in range(NRAW)]
        hi_split = sem("hi_split")
        chunk_split = sem("chunk_split")
        idle_set = sem("idle_set")
        chunk_used = sem("chunk_used")
        psum_full, psum_free = sem("psum_full"), sem("psum_free")
        x_in = [sem(f"x_in{n}") for n in range(len(X_PIECES))]
        consts_in, z_in, ln_in, table_in, rope_in, cache_in = (
            sem(n) for n in ("consts_in", "z_in", "ln_in", "table_in", "rope_in", "cache_in"))
        dve_step = sem("dve_step")
        act_done = sem("act_done")
        x_ready = sem("x_ready")
        h_ready = sem("h_ready")
        z_ready = sem("z_ready")
        root_asked = sem("root_asked")
        head_ready = sem("head_ready")
        packed = sem("packed")
        keys_masked = sem("keys_masked")
        conv_ready = sem("conv_ready")
        state_in = [sem(f"state_in{i}") for i in range(4)]
        state_out = [sem(f"state_out{i}") for i in range(4)]
        z_saved, y_out, conv_out, sp_out = sem("z_saved"), sem("y_out"), sem("conv_out"), sem("sp_out")
        block = ctx.enter_context(nc.Block())

        def cols(k, w, of):
            return of[:, k * w:(k + 1) * w]

        def pair(b):
            return ps[:, b:b + 2, 0:HALF]

        def two(v):
            return v.rearrange("p (a b) -> p a b", a=2)

        def one(v):
            return v.rearrange("p o k -> p (o k)")

        def gated_parts(n):
            dp, pt = (n // 2, n % 2) if n < 4 else (n - 4, None)
            dvs = slice(2 * dp, 2 * dp + 2)
            if n < 4:
                def part(t):
                    return t[:, dvs, 256 * pt:256 * pt + 256].rearrange("p k (t r) -> p t k r", t=2)
                tmp = ogt[:, 512 * pt:512 * pt + 512].rearrange("p (t k r) -> p t k r", t=2, k=2)
                return part(ogh), part(ogl), tmp, part(sg)
            at = 1024 if n == 4 else 0
            return (ogh[:, dvs, NP:NT], ogl[:, dvs, NP:NT],
                    ogt[:, at:at + 256].rearrange("p (k r) -> p k r", k=2), sg[:, dvs, NP:NT])

        U_V, U_SC, U_G, U_O0, U_OP, U_G2 = 8, 18, 22, 26, 27, 31
        U_O1, U_S1A, U_G3, U_T, U_SP, U_OUT, U_S1B, U_S0 = 33, 34, 38, 40, 46, 48, 52, 72
        SKIPPED = U_S0 - U_S1B - 4 - (2 * KT - 4)
        assert U_S0 + 8 == HEAD_BANKS

        @block.sync
        def _(sync):
            def load(i, j):
                c = i * NRAW + j
                sync.dma_start(raw[:, j, :], one(a["weights"][bass.ds(c, 1)].rearrange("o p k -> p o k"))
                               ).then_inc(raw_loaded[j], 16)

            for j in range(NRAW):
                load(0, j)
            with sync.Fori(1, CHUNKS // NRAW) as i:
                for j in range(NRAW):
                    sync.wait_ge(chunk_split, i * NRAW + (j - NRAW + 1))
                    load(i, j)

        @block.gpsimd
        def _(pool):
            UN = max(NRAW, NSPL)
            assert UN % NRAW == 0 and UN % NSPL == 0 and CHUNKS % UN == 0

            def split(i, j, first=False):
                r, s = j % NRAW, j % NSPL
                pool.wait_ge(raw_loaded[r], i * (16 * UN // NRAW) + 16 * (j // NRAW + 1))
                if not first:
                    pool.wait_ge(chunk_used, i * UN + (j - NSPL + 1))
                pool.tensor_tensor(idle[:, :], idle[:, :], idle[:, :], ALU.mult)
                pool.tensor_scalar(wh[:, s, :], raw[:, r, :], 1.0, 1.0, ALU.mult, ALU.mult).then_inc(hi_split, 1)
                pool.wait_ge(hi_split, i * UN + (j + 1))
                pool.tensor_tensor(wl[:, s, :], raw[:, r, :], wh[:, s, :].bitcast(f32),
                                   ALU.subtract).then_inc(chunk_split, 1)

            pool.memset(idle[:, :], 0.0).then_inc(idle_set, 1)
            pool.wait_ge(idle_set, 1)
            for j in range(UN):
                split(0, j, first=j < NSPL)
            with pool.Fori(1, CHUNKS // UN) as i:
                for j in range(UN):
                    split(i, j)

        @block.tensor
        def _(pe):
            ck, bk, hr, zr, hd, kc = (Count() for _ in range(6))
            owed = [False]

            def loop(times, counts, pers, body, peel=0):
                def checked(i):
                    before = owed[0]
                    body(i)
                    assert isinstance(i, int) or owed[0] == before
                repeat(pe, times, counts, pers, checked, peel)

            def mm(out, lhs, rhs, start, stop):
                ins = nc.tensor.matmul(out, lhs, rhs, start=start, stop=stop)
                if owed[0]:
                    owed[0] = False
                    ins.then_inc(chunk_used, 1)
                return ins

            def mm3(out, lhs, rhs, start, stop):
                mm(out, lhs[1], rhs[0], start, False)
                mm(out, lhs[0], rhs[1], False, False)
                return mm(out, lhs[0], rhs[0], False, stop)

            def bank(n=1):
                b = bk.at % 8
                if bk.past(8):
                    pe.wait_ge(psum_free, bk(n - 8))
                bk.add(n)
                return b

            def chunk():
                s = ck.at % NSPL
                ck.add()
                pe.wait_ge(chunk_split, ck())
                return s

            def unit(w_of, x_hi, x_lo, kts, x_wait=None, skipped=0):
                b = bank(2)
                for half in range(2):
                    c = slice(half * HALF, (half + 1) * HALF)
                    for k in range(kts):
                        if x_wait:
                            x_wait(half, k)
                        last = mm3(ps[:, b + half, 0:HALF], w_of(k), (x_hi[:, k, c], x_lo[:, k, c]),
                                   k == 0, k == kts - 1)
                    last.then_inc(psum_full, 1 + (skipped if half else 0))

            def by_halves(own, w_ofs, x, kts, before_half, chunk_each=False):
                for half in range(2):
                    before_half(half)
                    c = slice(half * HALF, (half + 1) * HALF)
                    for u, w_of in enumerate(w_ofs):
                        for k in range(kts):
                            last = mm3(ps[:, (own + 2 * u) % 8 + half, 0:HALF], w_of(k),
                                       (x[0][:, k, c], x[1][:, k, c]), k == 0, k == kts - 1)
                        if half == 1:
                            last.then_inc(psum_full, 2)
                            owed[0] = chunk_each

            def unit_of_chunk(x_hi=xh, x_lo=xl, x_wait=None):
                s = chunk()
                unit(lambda k: (cols(k, 128, wh[:, s, :]), cols(k, 128, wl[:, s, :])), x_hi, x_lo, KT, x_wait)
                owed[0] = True

            def natural(n_chunks, l_hi, l_lo, before=None, ends_stage=False):
                b0 = bk.at

                def product(s, k, t):
                    if k == 0:
                        bank()
                    tok, kk = slice(t * 128, (t + 1) * 128), k % 2
                    last = mm3(ps[:, (b0 + t) % 8, :], (l_hi[:, k, tok], l_lo[:, k, tok]),
                               (cols(kk, 512, wh[:, s, :]), cols(kk, 512, wl[:, s, :])),
                               k == 0, k == 2 * n_chunks - 1)
                    if k == 2 * n_chunks - 1:
                        last.then_inc(psum_full, 1)

                for c in range(n_chunks - 2 * ends_stage):
                    s = chunk()
                    if before:
                        before(c)
                    for kk in range(2):
                        for t in range(TT):
                            product(s, 2 * c + kk, t)
                    owed[0] = True
                if ends_stage:
                    slots = []
                    for tiles in (range(EARLY), range(EARLY, TT)):
                        for n in range(2):
                            c = n_chunks - 2 + n
                            if tiles[0] == 0:
                                slots.append(chunk())
                                before(c)
                            for t in tiles:
                                for kk in range(2):
                                    product(slots[n], 2 * c + kk, t)
                            owed[0] = tiles[0] > 0

            def x_piece(half, k):
                for n, (h, ks) in enumerate(X_PIECES):
                    if (half, k) == (h, ks[0]):
                        pe.wait_ge(x_ready, n + 1)

            def ffn(first):
                for g, tiles in enumerate(GROUPS):
                    def up(i):
                        starts = not first and g == 0 and isinstance(i, int)
                        if starts:
                            first_units()
                        for u in range(2 * starts, 4):
                            loads = first and g == 0 and isinstance(i, int) and u == 0
                            unit_of_chunk(x_wait=x_piece if loads else None)
                    loop(tiles // 2, (ck, bk), (4, 8), up, peel=int(g == 0))
                    h0 = hr.at
                    for half in range(2):
                        natural(tiles // 2, hh, hl, lambda c: pe.wait_ge(h_ready, h0 + 2 * c + 2),
                                ends_stage=g == 1 and half == 1)
                    hr.add(tiles)

            def to_T(tiles):
                for t in tiles:
                    zr.add()
                    pe.wait_ge(z_ready, zr())
                    for q in range(2):
                        b = bank()
                        for k in range(4):
                            last = nc.tensor.transpose(cols(k, 128, ps[:, b, :]),
                                                       cols(4 * q + k, 128, z[:, t, :]), ident[:, :])
                            if owed[0]:
                                owed[0] = False
                                last.then_inc(chunk_used, 1)
                        last.then_inc(psum_full, 1)
                pe.wait_ge(psum_free, bk())

            def begin_stage():
                to_T(range(EARLY))
                bk.add(2 * (TT - EARLY))

            def first_units():
                own = bk.at
                w_ofs = [lambda k, s=s: (cols(k, 128, wh[:, s, :]), cols(k, 128, wl[:, s, :]))
                         for s in (chunk(), chunk())]

                def before_half(half):
                    if half == 1:
                        bk.at = own - 2 * (TT - EARLY)
                        to_T(range(EARLY, TT))
                        bk.add(4)
                by_halves(own, w_ofs, (xh, xl), KT, before_half, chunk_each=True)

            def transposed(srcs, done=True):
                b = bank()
                for k, src in enumerate(srcs):
                    last = nc.tensor.transpose(cols(k, 128, ps[:, b, :]), src, ident[:, :])
                    if owed[0]:
                        owed[0] = False
                        last.then_inc(chunk_used, 1)
                last.then_inc(psum_full, 1)

            def head_wait():
                hd.add()
                pe.wait_ge(head_ready, hd())

            def state_products(group, slots):
                for bb in slots:
                    kc.add()
                    pe.wait_ge(keys_masked, kc())
                    for d in range(2):
                        b = bank()
                        last = mm(ps[:, b, :], km[:, bb, d * 128:(d + 1) * 128],
                                  vp[:, (4 * group + bb) // 2, :], True, True)
                    last.then_inc(psum_full, 2)

            def cross(group, i):
                b = bank()
                for bb in range(4):
                    pe.wait_ge(state_in[bb], i * 48 + 16 * (group + 1))
                for d in range(2):
                    for bb in range(4):
                        s = 16 * (4 * group + bb)
                        mm(ps[32 * bb:32 * bb + 32, b, :], qx[:, d, s:s + 32], cols(d, DV, state[:, bb, :]),
                           d == 0, False)
                for bb in range(4):
                    s = SC0[4] + 16 * (4 * group + bb)
                    last = mm(ps[32 * bb:32 * bb + 32, b, :], sc[:, s:s + 32], vs[:, :], False, True)
                last.then_inc(psum_full, 1)

            def head(i):
                u0 = bk.at
                starts = isinstance(i, int)
                if starts:
                    first_units()
                for _ in range(2 * starts, 4):
                    unit_of_chunk()
                natural(4, xh, xl)
                head_wait()
                for t in range(TT):
                    transposed([rot[:, k, t * 128:(t + 1) * 128] for k in range(2)])
                for j in range(TT):
                    if j != 4:
                        b = bank()
                    at, q0, n = (0, j * 128, NP - j * 128) if j < 3 else ((j - 3) * 256, (j - 1) * 128, 256)
                    kt = slice(j * 128, (j + 1) * 128)
                    for d in range(2):
                        last = mm3(ps[:, b, at:at + n], (kh[:, d, kt], kl[:, d, kt]),
                                   (qh[:, d, q0:q0 + n], ql[:, d, q0:q0 + n]), d == 0, d == 1)
                    if j != 3:
                        last.then_inc(psum_full, 1)
                for _ in range(2):
                    unit_of_chunk()
                head_wait()
                assert bk.at - u0 == U_O0
                cross(0, i)
                for t in range(PT):
                    b = bank()
                    for j in range(t + 1):
                        c = SC0[j] + (t - j) * 128
                        last = mm3(ps[:, b, :], (sch[:, c:c + 128], scl[:, c:c + 128]),
                                   (vh[:, j, :], vl[:, j, :]), j == 0, j == t)
                    last.then_inc(psum_full, 1)
                assert bk.at - u0 == U_G2
                unit_of_chunk()
                cross(1, i)
                assert bk.at - u0 == U_S1A
                state_products(1, (0, 1))
                unit_of_chunk()
                assert bk.at - u0 == U_T
                pe.wait_ge(psum_free, bk(U_O1 + 1 - U_T))
                for dp in range(2):
                    for t in range(0, PT, 2):
                        transposed([cols(2 * dp + k, 128, on[:, 1 + t + n, :]) for n in range(2) for k in range(2)])
                for dp in range(2):
                    transposed([cols(2 * dp + k, 128, o) for k in range(2) for o in (on[:, 0, :], on5[:, :])])
                for d in range(2):
                    b = bank()
                    c = slice(d * 128, (d + 1) * 128)
                    for j in range(PT):
                        last = mm3(ps[:, b, :], (knh[:, j, c], knl[:, j, c]), (vh[:, j, :], vl[:, j, :]),
                                   j == 0, j == PT - 1)
                    last.then_inc(psum_full, 1)
                assert bk.at - u0 == U_OUT

                for m in range(4):
                    s = chunk()
                    w_ofs = [lambda k, u=u: (cols(2 * k + u, 128, wh[:, s, :]), cols(2 * k + u, 128, wl[:, s, :]))
                             for u in range(2)]
                    if m == 0:
                        bank(4)
                        by_halves(bk.at - 4, w_ofs, (ogh, ogl), 4, lambda half: head_wait())
                    else:
                        for w_of in w_ofs:
                            unit(w_of, ogh, ogl, 4, skipped=SKIPPED if m == 3 and w_of is w_ofs[1] else 0)
                    owed[0] = True
                    if m == 0:
                        state_products(1, (2, 3))
                bk.add(SKIPPED)
                state_products(0, range(4))

            ffn(True)
            pe.wait_ge(consts_in, 32)
            begin_stage()
            loop(H, (ck, bk, hd, kc), (HEAD_CHUNKS, HEAD_BANKS, 4, 8), head, peel=1)

            def conv(i):
                for _ in range(12):
                    unit_of_chunk()
            loop(2, (ck, bk), (12, 24), conv, peel=1)

            def merge(i):
                for _ in range(4):
                    unit_of_chunk()
                    unit_of_chunk()
                    pe.wait_ge(conv_ready, KT)
                    unit_of_chunk(zh, zl)
            loop(2, (ck, bk), (12, 24), merge)
            for half in range(2):
                natural(4, mh, ml, lambda c: pe.wait_ge(conv_ready, KT + 2 * c + 2), ends_stage=half == 1)
            begin_stage()
            ffn(False)
            assert ck.at == CHUNKS

        @block.scalar
        def _(act):
            bk, root, ad, sn = Count(), Count(), Count(), Count()

            def result(ins):
                ad.add()
                ins.then_inc(act_done, 1)

            def copy(out, in_, **kw):
                return nc.scalar.activation(out, in_, ACT.Copy, **kw)

            def full(n=1):
                b = bk.at % 8
                bk.add(n)
                act.wait_ge(psum_full, bk())
                return b

            def ln_load(k):
                act.dma_start(lng[:, :], a[f"ln{k}_g"].to_broadcast([128, D])).then_inc(ln_in, 16)
                act.dma_start(lnb[:, :], a[f"ln{k}_b"].to_broadcast([128, D])).then_inc(ln_in, 16)

            def ffn(peel):
                for g, tiles in enumerate(GROUPS):
                    def up(i):
                        for u in range(2):
                            b = full(2)
                            if bk.past(7):
                                act.wait_ge(psum_free, bk(-6))
                            result(nc.scalar.activation(two(sig[:, u, :]), pair(b), ACT.Sigmoid))
                            bk.add(2)
                    repeat(act, tiles // 2, (bk, ad), (8, 2), up, peel=peel if g == 0 else 0)
                    bk.add(2 * TT)

            def roots(c0, c1):
                root.add()
                act.wait_ge(root_asked, root())
                result(nc.scalar.activation(rt[:, 1, c0:c1], rt[:, 0, c0:c1], ACT.Sqrt))

            def roots_and_to_T():
                for tiles in (range(EARLY), range(EARLY, TT)):
                    roots(tiles[0], tiles[-1] + 1)
                    to_T(tiles)

            def to_T(tiles):
                for t in tiles:
                    for q in range(2):
                        b = full()
                        result(copy(xh[:, 4 * q:4 * q + 4, t * 128:(t + 1) * 128],
                                    ps[:, b, :].rearrange("p (a b) -> p a b", a=4)))

            for n, (half, ks) in enumerate(X_PIECES):
                c, f = slice(half * HALF, (half + 1) * HALF), slice(ks[0], ks[-1] + 1)
                act.dma_start(xin[:, f, c], a["x_T"][:, f, c]).then_inc(x_in[n], 16)
            act.dma_start(z[:, 0:PT, :], a["x_prompt"].rearrange("(t p) d -> p t d", p=128)).then_inc(z_in, 16)
            act.dma_start(z[:, PT, :], a["x_sample"]).then_inc(z_in, 16)
            act.dma_start(ident[:, :], a["ident"]).then_inc(consts_in, 16)
            act.dma_start(odd_even[:, :], a["odd_even"]).then_inc(consts_in, 16)
            act.dma_start(convw[:, :, :], a["conv_w"]).then_inc(cache_in, 16)
            act.dma_start(cache[:, :, :, :], a["cache"]).then_inc(cache_in, 16)
            ln_load(1)
            ffn(1)
            roots_and_to_T()
            act.wait_ge(z_ready, TT)
            act.dma_start(a["z_scratch"], z[:, :, :]).then_inc(z_saved, 16)
            act.dma_start(cos[:, :], a["cos"]).then_inc(rope_in, 16)
            act.dma_start(sin[:, :], a["sin"]).then_inc(rope_in, 16)
            act.wait_ge(consts_in, 32)

            def dram_state(t, group, slot, i):
                return a[t][4 * group + slot, bass.ds(i, 1)].rearrange("o (k p) e -> p (o k) e", p=128)

            def state_load(i, group):
                for slot in range(4):
                    act.dma_start(state[:, slot, :].rearrange("p (k e) -> p k e", k=2),
                                  dram_state("state_ret", group, slot, i)).then_inc(state_in[slot], 16)

            def pack(i, out, parts):
                for n, part in enumerate(parts):
                    for g in range(4):
                        copy(out[32 * n:32 * n + 32, g, :], part[32 * g:32 * g + 32, :].bitcast(f32)
                             ).then_inc(packed, 1)

            def masked_keys(group):
                for bb in range(4):
                    st = 4 * group + bb
                    copy(km[:, bb, :], kp[:, st // 2, :].bitcast(f32),
                         scale=odd_even[:, st % 2:st % 2 + 1]).then_inc(keys_masked, 1)

            def state_store(i, group, slots, use):
                for n, slot in enumerate(slots):
                    act.wait_ge(psum_free, bk(use + 2 * n + 2 - bk.at))
                    act.dma_start(dram_state("ret_sample", group, slot, i),
                                  state[:, slot, :].rearrange("p (k e) -> p k e", k=2)
                                  ).then_inc(state_out[slot], 16)

            def head(i):
                u0 = bk.at
                if not isinstance(i, int):
                    act.wait_ge(psum_free, bk())
                    for slot in range(4):
                        act.wait_ge(state_out[slot], i * 32)
                act.dma_start(ht[:, :], one(a["tables"][bass.ds(i, 1)].rearrange("o p k -> p o k"))
                              ).then_inc(table_in, 16)
                state_load(i, 0)
                bk.add(U_V)
                for t in range(TT):
                    b = full()
                    result(copy(vh[:, t, :] if t < PT else v4[0][:, :], ps[:, b, :]))
                result(copy(vs[:, :], ps[:, b, :]))
                act.wait_ge(table_in, i * 16 + 16)
                for t in range(TT):
                    b = full()
                    if t >= 2:
                        act.wait_ge(psum_free, bk(-2))
                    result(copy(kd[:, t % 2, :], ps[:, b, 0:DK], scale=ht[:, HT_K + t:HT_K + t + 1]))
                act.wait_ge(psum_free, bk())
                pack(i, vp, (v4[0], v4[1], v4[0]))
                pack(i, kp, (k4[0], k4[0], k4[1]))
                act.wait_ge(packed, i * 24 + 24)
                masked_keys(1)
                bk.add(U_G - U_SC)

                def gate(u):
                    b = full(2)
                    result(nc.scalar.activation(two(sg[:, u, :]), pair(b), ACT.Sigmoid))

                gate(0)
                gate(1)
                full()
                state_load(i, 1)
                roots(0, 5)
                bk.add(U_G2 - U_OP)
                gate(2)
                roots(5, 6)
                bk.add(U_G3 - U_O1)
                for half in range(2):
                    act.wait_ge(psum_full, bk(1 + half))
                    result(nc.scalar.activation(cols(half, HALF, sg[:, 3, :]), ps[:, bk.at % 8 + half, 0:HALF],
                                                ACT.Sigmoid))
                bk.add(2)
                state_store(i, 1, (0, 1), u0 + U_S1A)
                for n in range(6):
                    act.wait_ge(psum_free, bk(1))
                    hi, _, tmp, _ = gated_parts(n)
                    result(copy(hi, tmp))
                    bk.add(1)
                act.wait_ge(psum_free, bk(U_OUT - U_SP))
                act.dma_start(a["ret_prompt"][bass.ds(i, 1)].rearrange("o (k p) e -> p (o k) e", p=128),
                              sp[:, :, :]).then_inc(sp_out, 16)
                act.wait_ge(psum_full, bk(U_S1B + 4 - U_SP))
                masked_keys(0)
                state_store(i, 1, (2, 3), u0 + U_S1B)
                for slot in range(4):
                    act.wait_ge(state_out[slot], i * 32 + 16)
                state_load(i, 0)
                state_store(i, 0, range(4), u0 + U_S0)
                bk.add(u0 + HEAD_BANKS - bk.at)

            repeat(act, H, (bk, ad, root), (HEAD_BANKS, 6 + 5 + 5 + 2 + 6, 2), head, peel=1)
            act.wait_ge(psum_free, bk())
            ln_load(2)

            def conv(i):
                for j in range(4):
                    b = full(2)
                    act.wait_ge(psum_free, bk(-8))
                    result(copy(two(csb[:, j % 2, :]), pair(b)))
                    bk.add(4)
            repeat(act, 2, (bk, ad), (24, 4), conv)

            def merge(i):
                for j in range(4):
                    b = full(2)
                    act.wait_ge(psum_free, bk(-8))
                    nc.scalar.activation(two(csb[:, j % 2, :]), pair(b), ACT.Sigmoid)
                    b = full(2)
                    result(nc.scalar.activation(two(cy[:, j % 2, :]), pair(b), ACT.Sigmoid))
                    bk.add(2)
            repeat(act, 2, (bk, ad), (24, 4), merge)
            act.wait_ge(z_saved, 16)
            act.wait_ge(psum_free, bk())
            act.dma_start(z[:, :, :], a["z_scratch"]).then_inc(z_in, 16)
            act.dma_start(a["conv_state"], cout[:, :, :, :]).then_inc(conv_out, 16)
            bk.add(2 * TT)
            roots_and_to_T()
            act.wait_ge(z_ready, 2 * TT)
            ln_load(3)
            ffn(0)
            roots(0, EARLY)
            roots(EARLY, TT)
            for t in range(TT):
                act.wait_ge(z_ready, 2 * TT + t + 1)
                dst = a["y_prompt"][t * 128:(t + 1) * 128, :] if t < PT else a["y_sample"]
                act.dma_start(dst, z[:, t, :]).then_inc(y_out, 16)
            act.wait_ge(y_out, 16 * TT)
            act.wait_ge(conv_out, 16)
            act.wait_ge(sp_out, 16 * H)
            for slot in range(4):
                act.wait_ge(state_out[slot], 32 * H)

        @block.vector
        def _(dve):
            bk, ad, st, hr, zr, root = (Count() for _ in range(6))
            V = nc.vector

            def step(ins):
                st.add()
                ins.then_inc(dve_step, 1)

            def after():
                dve.wait_ge(dve_step, st())

            def full(n=1):
                b = bk.at % 8
                bk.add(n)
                dve.wait_ge(psum_full, bk())
                return b

            def act_result(n=1):
                ad.add(n)
                dve.wait_ge(act_done, ad())

            def tt(out, x, y, op):
                return V.tensor_tensor(out, x, y, op)

            def split(hi, lo, x):
                step(V.tensor_copy(hi, x))
                after()
                return tt(lo, x, hi.bitcast(f32), ALU.subtract)

            def ffn():
                for g, tiles in enumerate(GROUPS):
                    def up(i):
                        for u in range(2):
                            act_result()
                            b = full(2)
                            s = two(sig[:, u, :])
                            tt(s, pair(b), s, ALU.mult).then_inc(psum_free, 2)
                            dve.wait_ge(psum_free, bk())
                            b = full(2)
                            tt(two(h32[:, u, :]), pair(b), s, ALU.mult).then_inc(psum_free, 2)
                            dve.wait_ge(psum_free, bk())
                            f = bass.ds(i * 2 + u, 1)
                            split(one(hh[:, f, :]), one(hl[:, f, :]), h32[:, u, :]).then_inc(h_ready, 1)
                    repeat(dve, tiles // 2, (bk, ad, st), (8, 2, 2), up, peel=0)
                    hr.add(tiles)
                    down(0.5 / ALPHA, 0)
                    if g == 0:
                        down(0.5 / ALPHA, 1)

            def down(scale, half, tiles=range(TT)):
                for t in tiles:
                    b = full()
                    zt = cols(half, 512, z[:, t, :])
                    V.scalar_tensor_tensor(out=zt, in0=ps[:, b, :], scalar=scale, in1=zt,
                                           op0=ALU.mult, op1=ALU.add).then_inc(psum_free, 1)
                dve.wait_ge(psum_free, bk())

            def inv_root(c0, c1, eps):
                var, r, inv, t = mv[:, c0:c1, 1], rt[:, 1, c0:c1], rt[:, 2, c0:c1], rt[:, 3, c0:c1]
                root.add()
                V.tensor_scalar(rt[:, 0, c0:c1], var, eps, None, ALU.add).then_inc(root_asked, 1)
                act_result()
                step(V.reciprocal(inv, r))
                after()
                step(tt(t, inv, inv, ALU.mult))
                after()
                step(tt(t, t, rt[:, 0, c0:c1], ALU.mult))
                after()
                step(V.tensor_scalar(t, t, -0.5, 1.5, ALU.mult, ALU.add))
                after()
                step(tt(inv, inv, t, ALU.mult))
                after()

            def moments(half, tiles):
                for t in tiles:
                    step(V.bn_stats(stats[:, t, 6 * half:6 * half + 6], cols(half, 512, z[:, t, :])))

            def inv_deviation(tiles):
                after()
                for t in tiles:
                    step(V.bn_aggr(mv[:, t, :], stats[:, t, :]))
                after()
                inv_root(tiles[0], tiles[-1] + 1, LN_EPS / ALPHA ** 2)

            def scale_and_shift(tiles):
                for t in tiles:
                    step(V.scalar_tensor_tensor(out=z[:, t, :], in0=z[:, t, :], scalar=mv[:, t, 0:1],
                                                in1=lng[:, :], op0=ALU.subtract, op1=ALU.mult))
                    after()
                    V.scalar_tensor_tensor(out=z[:, t, :], in0=z[:, t, :], scalar=rt[:, 2, t:t + 1],
                                           in1=lnb[:, :], op0=ALU.mult, op1=ALU.add).then_inc(z_ready, 1)

            def end_stage(k, scale, transpose=True):
                early, late = range(EARLY), range(EARLY, TT)
                moments(0, range(TT))
                for t in early:
                    down(scale, 1, [t])
                    moments(1, [t])
                inv_deviation(early)
                dve.wait_ge(ln_in, 32 * k)
                scale_and_shift(early[:2])
                down(scale, 1, late)
                scale_and_shift(early[2:])
                if transpose:
                    to_T(early)
                moments(1, late)
                inv_deviation(late)
                scale_and_shift(late)
                if transpose:
                    to_T(late)

            def to_T(tiles):
                for t in tiles:
                    for q in range(2):
                        b = full()
                        act_result()
                        part = slice(4 * q, 4 * q + 4), slice(t * 128, (t + 1) * 128)
                        tt(xl[:, part[0], part[1]], ps[:, b, :].rearrange("p (a b) -> p a b", a=4),
                           xh[:, part[0], part[1]].bitcast(f32), ALU.subtract).then_inc(psum_free, 1)

            for n, (half, ks) in enumerate(X_PIECES):
                c, f = slice(half * HALF, (half + 1) * HALF), slice(ks[0], ks[-1] + 1)
                dve.wait_ge(x_in[n], 16)
                split(xh[:, f, c], xl[:, f, c], xin[:, f, c]).then_inc(x_ready, 1)
            dve.wait_ge(z_in, 32)
            ffn()
            end_stage(1, 0.5 / ALPHA)

            dve.wait_ge(z_saved, 16)
            step(V.memset(yr, 0.0))
            step(V.memset(qx[:, :, 128:144], 0.0))
            step(V.memset(sc[:, 1408:1424], 0.0))
            step(V.memset(vp[96:128, :, :].bitcast(f32), 0.0))
            step(V.memset(kp[96:128, :, :].bitcast(f32), 0.0))
            dve.wait_ge(rope_in, 32)

            def rotate(hi, lo):
                b = full(2)
                step(tt(two(rope[:, 0, :]), pair(b), two(cos[:, :]), ALU.mult))
                tt(two(rope[:, 1, :]), pair(b), two(sin[:, :]), ALU.mult).then_inc(psum_free, 2)
                b = full(2)
                after()
                step(tt(two(rot[:, 0, :]), pair(b), two(sin[:, :]), ALU.mult))
                tt(two(rot[:, 1, :]), pair(b), two(cos[:, :]), ALU.mult).then_inc(psum_free, 2)
                after()
                dve.wait_ge(psum_free, bk())
                step(tt(rot[:, 0, :], rope[:, 0, :], rot[:, 0, :], ALU.subtract))
                step(tt(rot[:, 1, :], rope[:, 1, :], rot[:, 1, :], ALU.add))
                after()
                return split(hi[:, :, :], lo[:, :, :], rot[:, :, :])

            def normalise(b, c, out):
                V.tensor_scalar(out, ps[:, b, :], mv[:, c, 0:1], rt[:, 2, c:c + 1],
                                ALU.subtract, ALU.mult).then_inc(psum_free, 1)

            def signal_head():
                after()
                V.memset(rt[:, 3, 5:6], 0.0).then_inc(head_ready, 1)

            def gated(n):
                b = full()
                _, _, tmp, silu = gated_parts(n)
                if n < 4:
                    tt(tmp, ps[:, b, :].rearrange("p (t k r) -> p t k r", t=2, k=2), silu,
                       ALU.mult).then_inc(psum_free, 1)
                else:
                    tt(tmp.rearrange("p k (s r) -> p k s r", s=NS_),
                       ps[:, b, :].rearrange("p (k s r) -> p k s r", k=2, s=NS_)[:, :, :, 0:TS],
                       silu.rearrange("p k (s r) -> p k s r", s=NS_), ALU.mult).then_inc(psum_free, 1)

            def gated_lo(n):
                act_result()
                hi, lo, tmp, _ = gated_parts(n)
                step(tt(lo, tmp, hi.bitcast(f32), ALU.subtract))

            def head(i):
                u0 = bk.at
                dve.wait_ge(psum_full, bk(2))
                step(rotate(qh, ql))
                dve.wait_ge(table_in, i * 16 + 16)
                for d in range(2):
                    step(tt(qx[:, d, 0:128], rot[:, d, NP:NT], ht[:, HT_Q:HT_Q + 128], ALU.mult))
                rotate(kh, kl).then_inc(head_ready, 1)
                for t in range(TT):
                    b = full()
                    act_result(1 if t < PT else 2)
                    hi, lo = (vh[:, t, :], vl[:, t, :]) if t < PT else (v4[0][:, :], v4[1][:, :])
                    tt(lo, ps[:, b, :], hi.bitcast(f32), ALU.subtract).then_inc(psum_free, 1)
                for t in range(TT):
                    full()
                    act_result()
                    hi, lo = (knh[:, t, :], knl[:, t, :]) if t < PT else (k4[0][:, :], k4[1][:, :])
                    split(hi, lo, kd[:, t % 2, :]).then_inc(psum_free, 1)
                for j in range(3):
                    b = full()
                    n = NP - 128 * j
                    tt(sc[:, SC0[j]:SC0[j] + n], ps[:, b, 0:n], ht[:, HT_S:HT_S + n],
                       ALU.mult).then_inc(psum_free, 1)
                b = full()
                step(tt(sc[:, SC0[3]:SC0[3] + 128], ps[:, b, 128:256], ht[:, HT_S:HT_S + 128], ALU.mult))
                tt(sc[:, SC0[4]:SC0[4] + 128], ps[:, b, 384:512], ht[:, HT_M:HT_M + 128],
                   ALU.mult).then_inc(psum_free, 1)
                dve.wait_ge(psum_free, bk())
                after()
                split(sch[:, :], scl[:, :], sc[:, 0:1280]).then_inc(head_ready, 1)
                def gate(u):
                    act_result()
                    b = full(2)
                    tt(two(sg[:, u, :]), pair(b), two(sg[:, u, :]), ALU.mult).then_inc(psum_free, 2)

                gate(0)
                gate(1)
                banks = []
                for c in range(5):
                    banks.append(full())
                    step(V.bn_stats(stats[:, c, 0:6], ps[:, banks[c], :]))
                after()
                V.memset(rt[:, 3, 0:1], 0.0)
                for c in range(5):
                    step(V.bn_aggr(mv[:, c, :], stats[:, c, 0:6]))
                after()
                inv_root(0, 5, GN_EPS)
                for c in range(5):
                    normalise(banks[c], c, on[:, c, :])
                gate(2)
                b = full()
                step(V.bn_stats(stats[:, 5, 0:6], ps[:, b, :]))
                after()
                V.memset(rt[:, 3, 5:6], 0.0)
                step(V.bn_aggr(mv[:, 5, :], stats[:, 5, 0:6]))
                after()
                inv_root(5, 6, GN_EPS)
                normalise(b, 5, on5[:, :])

                def new_state(slots, loads):
                    for slot in slots:
                        dve.wait_ge(state_in[slot], i * 48 + 16 * loads)
                        for d in range(2):
                            b = full()
                            s = cols(d, DV, state[:, slot, :])
                            V.scalar_tensor_tensor(out=s, in0=s, scalar=ht[:, HT_G:HT_G + 1], in1=ps[:, b, :],
                                                   op0=ALU.mult, op1=ALU.add).then_inc(psum_free, 1)
                new_state((0, 1), 2)
                for half in range(2):
                    act_result()
                    s, b = cols(half, HALF, sg[:, 3, :]), full()
                    tt(s, ps[:, b, 0:HALF], s, ALU.mult).then_inc(psum_free, 1)
                dve.wait_ge(psum_free, bk())
                gated(0)
                gated(1)
                gated_lo(0)
                after()
                gated(2)
                gated_lo(1)
                after()
                gated(3)
                gated_lo(2)
                gated(4)
                gated_lo(3)
                signal_head()
                gated(5)
                gated_lo(4)
                gated_lo(5)
                signal_head()
                if not isinstance(i, int):
                    dve.wait_ge(sp_out, i * 16)
                for d in range(2):
                    b = full()
                    V.tensor_copy(sp[:, d, :], ps[:, b, :]).then_inc(psum_free, 1)

                def branch(m, skipped=0):
                    b = full(2)
                    tt(two(yr[:, m, :]), pair(b), two(yr[:, m, :]), ALU.add).then_inc(psum_free, 2 + skipped)
                    bk.add(skipped)
                branch(0)
                branch(1)
                new_state((2, 3), 2)
                for m in range(2, KT):
                    branch(m, SKIPPED if m == KT - 1 else 0)
                new_state(range(4), 3)
            repeat(dve, H, (bk, ad, st, root), (HEAD_BANKS, 24, 48, 2), head, peel=1)

            for slot in range(4):
                dve.wait_ge(state_out[slot], 32 * H)
            dve.wait_ge(sp_out, 16 * H)
            dve.wait_ge(cache_in, 32)
            step(V.memset(upr[:, :, 0:2], 0.0))

            def conv(i):
                for jj in range(4):
                    s, j = jj % 2, i * 4 + jj
                    u, us, y = upr[:, s, :], usm[:, s * NS_:(s + 1) * NS_, :], cy[:, s, :]
                    ys = y[:, NP:NT].rearrange("p (s r) -> p s r", s=NS_)
                    full(2)
                    act_result()
                    b = full(2)
                    step(V.tensor_copy(us[:, :, 0:2],
                                       cache[:, bass.ds(j, 1), :, :].rearrange("p o s r -> p (o s) r")))
                    step(tt(u[:, 2:2 + HALF], csb[:, s, 0:HALF], ps[:, b, 0:HALF], ALU.mult))
                    step(tt(u[:, 2 + HALF:2 + NP], csb[:, s, HALF:NP], ps[:, b + 1, 0:NP - HALF], ALU.mult))
                    tt(us[:, :, 2:2 + TS], csb[:, s, NP:NT].rearrange("p (s r) -> p s r", s=NS_),
                       ps[:, b + 1, NP - HALF:HALF].rearrange("p (s r) -> p s r", s=NS_),
                       ALU.mult).then_inc(psum_free, 4)
                    after()
                    dve.wait_ge(psum_free, bk())

                    def w(n):
                        return convw[:, n, bass.ds(j, 1)]
                    step(V.tensor_scalar(y[:, 0:NP], u[:, 0:NP], w(0), None, ALU.mult))
                    step(V.tensor_scalar(ys, us[:, :, 0:TS], w(0), None, ALU.mult))
                    for n in (1, 2):
                        after()
                        for out, x in ((y[:, 0:NP], u[:, n:n + NP]), (ys, us[:, :, n:n + TS])):
                            step(V.scalar_tensor_tensor(out=out, in0=x, scalar=w(n), in1=out,
                                                        op0=ALU.mult, op1=ALU.add))
                    cj = cout[:, bass.ds(j, 1), :, :].rearrange("p o s r -> p (o s) r")
                    step(V.tensor_copy(cj[:, 0:1, :], u[:, NP:NP + 2].rearrange("p (o r) -> p o r", o=1)))
                    step(V.tensor_copy(cj[:, 1:1 + NS_, :], us[:, :, TS:TS + 2]))
                    after()
                    b = full(2)
                    tt(two(cz[:, 0, :]), pair(b), two(y), ALU.mult).then_inc(psum_free, 2)
                    dve.wait_ge(psum_free, bk())
                    f = bass.ds(j, 1)
                    split(one(zh[:, f, :]), one(zl[:, f, :]), cz[:, 0, :]).then_inc(conv_ready, 1)
            repeat(dve, 2, (bk, ad, st), (24, 4, 48), conv)

            def merge(i):
                for jj in range(4):
                    s, f = jj % 2, bass.ds(i * 4 + jj, 1)
                    full(4)
                    act_result()
                    dve.wait_ge(conv_ready, i * 4 + (KT + jj))
                    tt(cz[:, 0, :], cy[:, s, :], one(yr[:, f, :]), ALU.mult).then_inc(psum_free, 4)
                    dve.wait_ge(psum_free, bk())
                    b = full(2)
                    step(tt(two(csb[:, s, :]), pair(b), two(csb[:, s, :]), ALU.mult))
                    after()
                    tt(cz[:, 0, :], cz[:, 0, :], csb[:, s, :], ALU.add).then_inc(psum_free, 2)
                    dve.wait_ge(psum_free, bk())
                    split(one(mh[:, f, :]), one(ml[:, f, :]), cz[:, 0, :]).then_inc(conv_ready, 1)
            repeat(dve, 2, (bk, ad, st), (24, 4, 8), merge)
            dve.wait_ge(z_in, 48)
            down(1.0 / ALPHA, 0)
            end_stage(2, 1.0 / ALPHA)
            ffn()
            end_stage(3, 0.5 / ALPHA, transpose=False)


def decay_tables():
    f = np.float32
    lg = np.log(f(1.0) - f(2.0) ** (f(-5.0) - np.arange(H, dtype=f))).astype(f)
    k = np.arange(128)
    t = np.zeros((H, 128, HT_W), f)
    scale = f(DK ** -0.5)
    for h in range(H):
        diff = np.arange(NP)[None, :] - k[:, None]
        t[h, :, HT_S:HT_S + NP] = np.where(diff >= 0, np.exp(lg[h] * np.maximum(diff, 0).astype(f)), 0) * scale
        diff = k[None, :] - k[:, None]
        inside = (diff >= 0) & (k[None, :] // TS == k[:, None] // TS)
        t[h, :, HT_M:HT_M + 128] = np.where(inside, np.exp(lg[h] * np.maximum(diff, 0).astype(f)), 0) * scale
        t[h, :, HT_Q:HT_Q + 128] = np.exp(lg[h] * (k % TS + 1).astype(f))[None, :]
        for tile in range(PT):
            t[h, :, HT_K + tile] = np.exp(lg[h] * (NP - 1 - (tile * 128 + k)).astype(f)) * scale
        t[h, :, HT_K + PT] = np.exp(lg[h] * (TS - 1 - k % TS).astype(f)) * scale
        t[h, :, HT_G] = np.exp(lg[h] * f(TS))
    return t


def rope_tables():
    f = np.float32
    half = DK // 2
    inv = (f(ROPE_BASE) ** (-np.arange(half, dtype=f) / f(half))).astype(f)
    pos = np.concatenate([np.arange(NP), np.tile(PAST_LEN + np.arange(TS), NS_)]).astype(f)
    ang = (inv[:, None] * pos[None, :]).astype(f)
    return np.cos(ang).astype(f), np.sin(ang).astype(f)


def weight_chunks(ffn1_up, ffn1_down, w_in, w_conv, w_ret, w_out, ffn2_up, ffn2_down):
    out = []

    def tiled(w, cols):
        return w.reshape(-1, 128, cols).transpose(1, 0, 2).reshape(128, -1)

    def t_unit(w, c):
        out.append(tiled(w[:, c:c + 128], 128))

    def natural(w, c, k0, k1):
        for k in range(k0, k1, 2):
            out.append(tiled(w[k * 128:(k + 2) * 128, c:c + 512], 512))

    def ffn(up, down):
        f0 = 0
        for tiles in GROUPS:
            for f in range(f0, f0 + tiles):
                t_unit(up, f * 128)
                t_unit(up, D_FF + f * 128)
            for half in range(2):
                natural(down, half * 512, f0, f0 + tiles)
            f0 += tiles

    cb, cc, ch, q, k, v, g, gc, gr = np.cumsum([0, D, D, D, H * DK, H * DK, H * DV, H * DV, D])
    ffn(ffn1_up, ffn1_down)
    for h in range(H):
        for first in (q + h * DK, k + h * DK):
            t_unit(w_in, first)
            t_unit(w_in, first + 128)
        natural(w_in, v + h * DV, 0, KT)
        for u in range(4):
            t_unit(w_in, g + h * DV + u * 128)
        for m in range(4):
            out.append(tiled(w_ret[h * DV:(h + 1) * DV, m * 256:(m + 1) * 256], 256))
    for j in range(KT):
        for first in (cc, ch, cb):
            t_unit(w_in, first + j * 128)
    for j in range(KT):
        t_unit(w_in, gc + j * 128)
        t_unit(w_in, gr + j * 128)
        t_unit(w_conv, j * 128)
    for half in range(2):
        natural(w_out, half * 512, 0, KT)
    ffn(ffn2_up, ffn2_down)
    return np.stack(out)


def kernel(x_prompt, x_sample, cache_conv, state_ret, ln1_g, ln1_b, ffn1_w_up, ffn1_w_down, w_in, conv_w,
           w_conv_br, w_ret_br, w_out, ln2_g, ln2_b, ffn2_w_up, ffn2_w_down, ln3_g, ln3_b):
    import concourse.bacc as bacc
    from concourse.bass_utils import run_bass_kernel_spmd

    def arr(v):
        return np.ascontiguousarray(np.asarray(v))

    xp, xs = arr(x_prompt)[0], arr(x_sample).reshape(NS_ * TS, D)
    x = np.concatenate([xp, xs])
    cos, sin = rope_tables()
    ins = {
        "x_T": x.T.reshape(KT, 128, NT).transpose(1, 0, 2),
        "x_prompt": xp,
        "x_sample": xs,
        "state_ret": arr(state_ret)[0],
        "cache": arr(cache_conv)[0].reshape(NS_, 2, KT, 128).transpose(3, 2, 0, 1),
        "conv_w": arr(conv_w)[0].reshape(3, KT, 128).transpose(2, 0, 1),
        "weights": weight_chunks(*(arr(w)[0] for w in (ffn1_w_up, ffn1_w_down, w_in, w_conv_br, w_ret_br,
                                                       w_out, ffn2_w_up, ffn2_w_down))),
        "ln1_g": arr(ln1_g), "ln1_b": arr(ln1_b), "ln2_g": arr(ln2_g), "ln2_b": arr(ln2_b),
        "ln3_g": arr(ln3_g), "ln3_b": arr(ln3_b),
        "cos": cos, "sin": sin, "tables": decay_tables(),
        "ident": np.eye(128, dtype=np.float32),
        "odd_even": ((np.arange(128)[:, None] // TS % 2 == np.arange(2)[None, :])
                     & (np.arange(128)[:, None] < 96)).astype(np.float32),
    }
    outs = {
        "y_prompt": (NP, D), "y_sample": (NS_ * TS, D), "conv_state": (128, KT, NS_ + 1, 2),
        "ret_prompt": (H, DK, DV), "ret_sample": (NS_, H, DK, DV),
    }
    ins = {k: np.ascontiguousarray(v) for k, v in ins.items()}
    nc = bacc.Bacc("TRN2", target_bir_lowering=False, num_devices=1)
    ins = {f"in_{k}": v for k, v in ins.items()}
    args = {k[3:]: nc.dram_tensor(k, v.shape, mybir.dt.float32, kind="ExternalInput").ap() for k, v in ins.items()}
    args |= {k: nc.dram_tensor(f"out_{k}", s, mybir.dt.float32, kind="ExternalOutput").ap() for k, s in outs.items()}
    args["z_scratch"] = nc.dram_tensor("z_scratch", (128, TT, D), mybir.dt.float32, kind="Internal").ap()
    build_layer(nc, args)
    r = run_bass_kernel_spmd(nc, [ins], core_ids=[0]).results[0]
    r = {k: r[f"out_{k}"] for k in outs}

    conv = r["conv_state"].transpose(2, 3, 1, 0).reshape(NS_ + 1, 2, D)
    return (r["y_prompt"][None], r["y_sample"].reshape(NS_, TS, D), conv[None, 0:1], r["ret_prompt"][None, None],
            conv[None, 1:], r["ret_sample"][None])
```
